# Optimizing a Trainium2 kernel written in Bass

```python
import math, functools
import numpy as np
import jax
import jax.numpy as jnp
from jax import lax

D_MODEL = 1024
BATCH = 1
SEQ = 256
DEPTH = 2
DEC_BATCH = 8
DEC_SEQ = 1
PAST_LEN = 256
PAGE_SIZE = 128

N_HEADS = 8
N_KV_HEADS = 2
HEAD_DIM = 64
GROUP = N_HEADS // N_KV_HEADS
Q_W = N_HEADS * HEAD_DIM
KV_W = N_KV_HEADS * HEAD_DIM
CMP_BLOCK = 32
CMP_STRIDE = 16
CMP_HIDDEN = 128
SEL_BLOCK = 64
N_SEL = 8
WINDOW = 512
Q_BLOCK = 128
ROPE_THETA = 10000.0
SSM_WIDTH = D_MODEL // 2
SSM_GROUP = 16
SSM_GROUPS = SSM_WIDTH // SSM_GROUP
SSM_STATE = 64
SSM_CHUNK = 128
D_FF = 11 * D_MODEL // 4
CONV_W = 3
PLE_DIM = 256
EPS = 1e-6
NEG_INF = -1e30
FORCE_SCORE = 1e9
SCALE = HEAD_DIM ** -0.5
SPLIT_SIZES = (Q_W, KV_W, KV_W, KV_W, KV_W, KV_W, KV_W, 3 * N_HEADS, SSM_WIDTH, D_MODEL, D_MODEL)
N_IN = sum(SPLIT_SIZES)

kernel_name = 'nsa_s5_hybrid_decode_step'

def rmsnorm(x, g):
    xf = x.astype(jnp.float32)
    y = xf * lax.rsqrt(jnp.mean(xf * xf, axis=-1, keepdims=True) + EPS)
    return (y * g.astype(jnp.float32)).astype(x.dtype)

def rope(x, pos):
    half = HEAD_DIM // 2
    inv = jnp.float32(ROPE_THETA) ** (-jnp.arange(half, dtype=jnp.float32) / half)
    ang = pos.astype(jnp.float32)[:, None] * inv[None, :]
    cos = jnp.cos(ang)[:, None, :]
    sin = jnp.sin(ang)[:, None, :]
    xf = x.astype(jnp.float32)
    x1, x2 = xf[..., :half], xf[..., half:]
    return jnp.concatenate([x1 * cos - x2 * sin, x2 * cos + x1 * sin], axis=-1).astype(x.dtype)

def masked_softmax(s, mask):
    s = jnp.where(mask, s.astype(jnp.float32), NEG_INF)
    m = jnp.max(s, axis=-1, keepdims=True)
    e = jnp.where(mask, jnp.exp(s - m), 0.0)
    return e / jnp.maximum(jnp.sum(e, axis=-1, keepdims=True), 1e-30)

def attend(q, k, v, mask):
    s = jnp.einsum('btkgd,bskd->bkgts', q, k) * SCALE
    p = masked_softmax(s, mask)
    o = jnp.einsum('bkgts,bskd->btkgd', p.astype(v.dtype), v)
    return o, p

def window_mask(q_pos, k_pos):
    d = q_pos[:, None] - k_pos[None, :]
    return (d >= 0) & (d < WINDOW) & (k_pos[None, :] >= 0)

def compress(x, w1, pe, w2):
    B, L, K, D = x.shape
    xt = x.transpose(0, 2, 1, 3).reshape(B * K, L, D)
    hdn = lax.conv_general_dilated(xt, w1.astype(xt.dtype), (CMP_STRIDE,), 'VALID',
                                   dimension_numbers=('NWC', 'WIO', 'NWC'))
    hdn = hdn + jnp.einsum('ld,ldf->f', pe, w1)
    out = jax.nn.gelu(hdn) @ w2
    n = out.shape[1]
    return out.reshape(B, K, n, D).transpose(0, 2, 1, 3)

def cmp_branch(q, kc_full, vc_full, q_pos, wk1, pek, wk2, wv1, pev, wv2):
    kcmp = compress(kc_full, wk1, pek, wk2)
    vcmp = compress(vc_full, wv1, pev, wv2)
    n_cmp = kcmp.shape[1]
    start = jnp.arange(n_cmp) * CMP_STRIDE
    end = start + CMP_BLOCK - 1
    kcmp = rope(kcmp, end)
    o, p = attend(q, kcmp, vcmp, end[None, :] <= q_pos[:, None])
    L = kc_full.shape[1]
    n_sb = -(-L // SEL_BLOCK)
    sb_start = jnp.arange(n_sb) * SEL_BLOCK
    overlap = ((start[:, None] < sb_start[None, :] + SEL_BLOCK) & (end[:, None] >= sb_start[None, :])).astype(jnp.float32)
    imp = jnp.einsum('bkgtn,nj->btkj', p, overlap)
    blk = jnp.arange(n_sb)
    forced = (blk[None, :] == 0) | (blk[None, :] == (q_pos // SEL_BLOCK)[:, None])
    causal = sb_start[None, :] <= q_pos[:, None]
    imp = jnp.where(forced[None, :, None, :], FORCE_SCORE, imp)
    imp = jnp.where(causal[None, :, None, :], imp, NEG_INF)
    top_v, top_i = lax.top_k(imp, min(N_SEL, n_sb))
    return o, top_i, top_v > 0.5 * NEG_INF

def sel_attend(q, idx, valid, q_pos, fetch):
    pos = idx[..., None] * SEL_BLOCK + jnp.arange(SEL_BLOCK)
    k, v = fetch(pos)
    B, Tc, K, N, S = pos.shape
    mask = (valid[..., None] & (pos <= q_pos[None, :, None, None, None])).reshape(B, Tc, K, N * S)
    k = k.reshape(B, Tc, K, N * S, HEAD_DIM)
    v = v.reshape(B, Tc, K, N * S, HEAD_DIM)
    s = jnp.einsum('btkgd,btksd->btkgs', q, k) * SCALE
    p = masked_softmax(s, mask[:, :, :, None, :])
    return jnp.einsum('btkgs,btksd->btkgd', p.astype(v.dtype), v)

def to_chunks(x, c):
    B, T = x.shape[:2]
    return x.reshape((B, T // c, c) + x.shape[2:]).swapaxes(0, 1)

def from_chunks(x):
    nc, B, c = x.shape[:3]
    return x.swapaxes(0, 1).reshape((B, nc * c) + x.shape[3:])

def batch_head_index(B):
    bi = jnp.arange(B)[:, None, None, None, None]
    hd = jnp.arange(N_KV_HEADS)[None, None, :, None, None]
    return bi, hd

def nsa_prompt(q, kc, vc, ks, vs, kw, vw, cmpw):
    B, T = q.shape[:2]
    pos = jnp.arange(T)
    o_cmp, idx, valid = cmp_branch(q, kc, vc, pos, *cmpw)
    bi, hd = batch_head_index(B)

    def fetch(p):
        pc = jnp.clip(p, 0, T - 1)
        return ks[bi, pc, hd], vs[bi, pc, hd]

    qb = Q_BLOCK if T % Q_BLOCK == 0 else T
    o_sel = from_chunks(lax.map(lambda a: sel_attend(a[0], a[1], a[2], a[3], fetch),
                                (to_chunks(q, qb), to_chunks(idx, qb), to_chunks(valid, qb), pos.reshape(-1, qb))))
    kp = jnp.pad(kw, ((0, 0), (WINDOW, 0), (0, 0), (0, 0)))
    vp = jnp.pad(vw, ((0, 0), (WINDOW, 0), (0, 0), (0, 0)))

    def win_block(a):
        c, qc = a
        start = c * qb
        kb = lax.dynamic_slice_in_dim(kp, start, WINDOW + qb, axis=1)
        vb = lax.dynamic_slice_in_dim(vp, start, WINDOW + qb, axis=1)
        qpos = start + jnp.arange(qb)
        kpos = start - WINDOW + jnp.arange(WINDOW + qb)
        return attend(qc, kb, vb, window_mask(qpos, kpos))[0]

    o_win = from_chunks(lax.map(win_block, (jnp.arange(T // qb), to_chunks(q, qb))))
    n_keep = min(WINDOW, T)
    rows = (jnp.stack([kc, vc], axis=2), jnp.stack([ks, vs], axis=2), jnp.stack([kw, vw], axis=2)[:, T - n_keep:])
    return o_cmp, o_sel, o_win, rows

def nsa_sample(q, kc, vc, ks, vs, kw, vw, cmpw, cmp_pool, sel_pool, win_buf, page_table):
    B, T = q.shape[:2]
    past = page_table.shape[1] * PAGE_SIZE
    pos = past + jnp.arange(T)
    past_cmp = cmp_pool[page_table].reshape((B, past) + cmp_pool.shape[2:])
    kc_full = jnp.concatenate([past_cmp[:, :, 0].astype(kc.dtype), kc], axis=1)
    vc_full = jnp.concatenate([past_cmp[:, :, 1].astype(vc.dtype), vc], axis=1)
    o_cmp, idx, valid = cmp_branch(q, kc_full, vc_full, pos, *cmpw)
    sel_rows = sel_pool.reshape((-1,) + sel_pool.shape[2:])
    bi, hd = batch_head_index(B)

    def fetch(p):
        pc = jnp.clip(p, 0, past - 1)
        phys = page_table[bi, pc // PAGE_SIZE] * PAGE_SIZE + pc % PAGE_SIZE
        pn = jnp.clip(p - past, 0, T - 1)
        in_past = (p < past)[..., None]
        k = jnp.where(in_past, sel_rows[phys, 0, hd].astype(ks.dtype), ks[bi, pn, hd])
        v = jnp.where(in_past, sel_rows[phys, 1, hd].astype(vs.dtype), vs[bi, pn, hd])
        return k, v

    o_sel = sel_attend(q, idx, valid, pos, fetch)
    wb = win_buf.shape[1]
    win_all = jnp.concatenate([win_buf.astype(kw.dtype), jnp.stack([kw, vw], axis=2)], axis=1)
    kpos = past - wb + jnp.arange(wb + T)
    o_win, _ = attend(q, win_all[:, :, 0], win_all[:, :, 1], window_mask(pos, kpos))
    rows = (jnp.stack([kc, vc], axis=2), jnp.stack([ks, vs], axis=2), win_all[:, T:])
    return o_cmp, o_sel, o_win, rows

def cmul_combine(e1, e2):
    ar1, ai1, br1, bi1 = e1
    ar2, ai2, br2, bi2 = e2
    return (ar2 * ar1 - ai2 * ai1, ar2 * ai1 + ai2 * ar1,
            ar2 * br1 - ai2 * bi1 + br2, ar2 * bi1 + ai2 * br1 + bi2)

def ssm_scan(u, h0_re, h0_im, a_re, a_im, log_dt, b_re, b_im, c_re, c_im, d_skip):
    B, T, _ = u.shape
    uf = u.astype(jnp.float32).reshape(B, T, SSM_GROUPS, SSM_GROUP)
    ar = a_re.astype(jnp.float32)
    ai = a_im.astype(jnp.float32)
    dt = jnp.exp(log_dt.astype(jnp.float32))[:, None]
    mag = jnp.exp(dt * ar)
    ab_re = mag * jnp.cos(dt * ai)
    ab_im = mag * jnp.sin(dt * ai)
    den = ar * ar + ai * ai
    zr = ((ab_re - 1.0) * ar + ab_im * ai) / den
    zi = (ab_im * ar - (ab_re - 1.0) * ai) / den
    br = b_re.astype(jnp.float32)
    bim = b_im.astype(jnp.float32)
    bb_re = zr[..., None] * br - zi[..., None] * bim
    bb_im = zr[..., None] * bim + zi[..., None] * br
    bu_re = jnp.einsum('gpc,btgc->tbgp', bb_re, uf)
    bu_im = jnp.einsum('gpc,btgc->tbgp', bb_im, uf)
    chunk = SSM_CHUNK if T % SSM_CHUNK == 0 else T
    nc = T // chunk
    shp = (chunk, B, SSM_GROUPS, SSM_STATE)
    bu_re = bu_re.reshape((nc,) + shp)
    bu_im = bu_im.reshape((nc,) + shp)
    a_re_c = jnp.broadcast_to(ab_re, shp)
    a_im_c = jnp.broadcast_to(ab_im, shp)
    cr = c_re.astype(jnp.float32)
    ci = c_im.astype(jnp.float32)

    def step(carry, xs):
        hr0, hi0 = carry
        xr, xi = xs
        pr, pim, sr, si = lax.associative_scan(cmul_combine, (a_re_c, a_im_c, xr, xi), axis=0)
        hr = sr + pr * hr0 - pim * hi0
        hi = si + pr * hi0 + pim * hr0
        y = jnp.einsum('gcp,tbgp->tbgc', cr, hr) - jnp.einsum('gcp,tbgp->tbgc', ci, hi)
        return (hr[-1], hi[-1]), y

    (hr, hi), y = lax.scan(step, (h0_re.astype(jnp.float32), h0_im.astype(jnp.float32)), (bu_re, bu_im))
    y = y.reshape(T, B, SSM_GROUPS, SSM_GROUP).transpose(1, 0, 2, 3) + d_skip.astype(jnp.float32) * uf
    return y.reshape(B, T, SSM_WIDTH).astype(u.dtype), hr.astype(h0_re.dtype), hi.astype(h0_im.dtype)

def block(h, p_l, pos, lw, nsa_fn, h0_re, h0_im, conv_prefix):
    (g_attn, w_in, g_q, g_kc, g_ks, g_kw, wk1, pek, wk2, wv1, pev, wv2,
     a_re, a_im, log_dt, b_re, b_im, c_re, c_im, d_skip,
     w_a, w_glu1, w_glu2, w_o, g_ffn, w_up, conv_w, conv_b, w_down,
     g_ple, w_ple_gate, w_ple) = lw
    B, T, _ = h.shape
    xn = rmsnorm(h, g_attn)
    z = xn @ w_in
    pts = [int(s) for s in np.cumsum(SPLIT_SIZES)[:-1]]
    q, kc, vc, ks, vs, kw, vw, gl, u, ga, gb = jnp.split(z, pts, axis=-1)

    def heads(t):
        return t.reshape(B, T, -1, HEAD_DIM)

    q = rope(rmsnorm(heads(q), g_q), pos).reshape(B, T, N_KV_HEADS, GROUP, HEAD_DIM)
    kc = rmsnorm(heads(kc), g_kc)
    ks = rope(rmsnorm(heads(ks), g_ks), pos)
    kw = rope(rmsnorm(heads(kw), g_kw), pos)
    vc, vs, vw = heads(vc), heads(vs), heads(vw)
    o_cmp, o_sel, o_win, rows = nsa_fn(q, kc, vc, ks, vs, kw, vw, (wk1, pek, wk2, wv1, pev, wv2))
    bg = jax.nn.sigmoid(gl).reshape(B, T, N_KV_HEADS, GROUP, 3)
    o = bg[..., 0:1] * o_cmp + bg[..., 1:2] * o_sel + bg[..., 2:3] * o_win
    a_out = o.reshape(B, T, Q_W) @ w_a
    y, hr, hi = ssm_scan(u, h0_re, h0_im, a_re, a_im, log_dt, b_re, b_im, c_re, c_im, d_skip)
    yg = jax.nn.gelu(y)
    b_out = (yg @ w_glu1) * jax.nn.sigmoid(yg @ w_glu2)
    h = h + (jax.nn.sigmoid(ga) * a_out + jax.nn.sigmoid(gb) * b_out) @ w_o
    up = rmsnorm(h, g_ffn) @ w_up
    gp, val = jnp.split(up, 2, axis=-1)
    ext = jnp.concatenate([conv_prefix.astype(gp.dtype), gp], axis=1)
    conv = conv_b
    for j in range(CONV_W):
        conv = conv + conv_w[j] * ext[:, j:j + T]
    h = h + (jax.nn.gelu(conv) * val) @ w_down
    h = h + jax.nn.sigmoid(rmsnorm(h, g_ple) @ w_ple_gate) * (p_l @ w_ple)
    return h, rows, hr, hi, ext[:, T:]

def setup_inputs(seed: int = 0) -> dict:
    key = jax.random.key(seed)
    ks = jax.random.split(key, 48)
    f32 = jnp.float32
    n_pages = PAST_LEN // PAGE_SIZE
    n_pool = (DEC_BATCH * n_pages * 5) // 4
    win_buf = min(WINDOW, PAST_LEN)
    kv_row = (2, N_KV_HEADS, HEAD_DIM)

    def nrm(i, shape, scale=1.0):
        return scale * jax.random.normal(ks[i], shape, f32)

    def gain(i, shape):
        return 1.0 + 0.05 * jax.random.normal(ks[i], shape, f32)

    page_table = jax.random.permutation(ks[8], n_pool)[:DEC_BATCH * n_pages].reshape(DEC_BATCH, n_pages).astype(jnp.int32)
    a_im = jnp.pi * jnp.arange(SSM_STATE, dtype=f32) + nrm(24, (DEPTH, SSM_GROUPS, SSM_STATE), 0.01)
    log_dt = math.log(1e-3) + (math.log(1e-1) - math.log(1e-3)) * jax.random.uniform(ks[25], (DEPTH, SSM_GROUPS), f32)
    return {
        'x_prompt': nrm(0, (BATCH, SEQ, D_MODEL)),
        'x_sample': nrm(1, (DEC_BATCH, DEC_SEQ, D_MODEL)),
        'cache_cmp': nrm(2, (DEPTH, n_pool, PAGE_SIZE) + kv_row),
        'cache_sel': nrm(3, (DEPTH, n_pool, PAGE_SIZE) + kv_row),
        'cache_win': nrm(4, (DEPTH, DEC_BATCH, win_buf) + kv_row),
        'state_ssm_re': nrm(5, (DEPTH, DEC_BATCH, SSM_GROUPS, SSM_STATE), 0.3),
        'state_ssm_im': nrm(6, (DEPTH, DEC_BATCH, SSM_GROUPS, SSM_STATE), 0.3),
        'state_conv': nrm(7, (DEPTH, DEC_BATCH, CONV_W - 1, D_FF)),
        'page_table': page_table,
        'p_prompt': nrm(9, (DEPTH, BATCH, SEQ, PLE_DIM)),
        'p_sample': nrm(10, (DEPTH, DEC_BATCH, DEC_SEQ, PLE_DIM)),
        'g_attn': gain(11, (DEPTH, D_MODEL)),
        'w_in': nrm(12, (DEPTH, D_MODEL, N_IN), D_MODEL ** -0.5),
        'g_q': gain(13, (DEPTH, HEAD_DIM)),
        'g_kc': gain(14, (DEPTH, HEAD_DIM)),
        'g_ks': gain(15, (DEPTH, HEAD_DIM)),
        'g_kw': gain(16, (DEPTH, HEAD_DIM)),
        'cmp_wk1': nrm(17, (DEPTH, CMP_BLOCK, HEAD_DIM, CMP_HIDDEN), (CMP_BLOCK * HEAD_DIM) ** -0.5),
        'cmp_pek': nrm(18, (DEPTH, CMP_BLOCK, HEAD_DIM), 0.1),
        'cmp_wk2': nrm(19, (DEPTH, CMP_HIDDEN, HEAD_DIM), CMP_HIDDEN ** -0.5),
        'cmp_wv1': nrm(20, (DEPTH, CMP_BLOCK, HEAD_DIM, CMP_HIDDEN), (CMP_BLOCK * HEAD_DIM) ** -0.5),
        'cmp_pev': nrm(21, (DEPTH, CMP_BLOCK, HEAD_DIM), 0.1),
        'cmp_wv2': nrm(22, (DEPTH, CMP_HIDDEN, HEAD_DIM), CMP_HIDDEN ** -0.5),
        'ssm_a_re': -0.5 + nrm(23, (DEPTH, SSM_GROUPS, SSM_STATE), 0.01),
        'ssm_a_im': a_im,
        'ssm_log_dt': log_dt,
        'ssm_b_re': nrm(26, (DEPTH, SSM_GROUPS, SSM_STATE, SSM_GROUP), (2 * SSM_GROUP) ** -0.5),
        'ssm_b_im': nrm(27, (DEPTH, SSM_GROUPS, SSM_STATE, SSM_GROUP), (2 * SSM_GROUP) ** -0.5),
        'ssm_c_re': nrm(28, (DEPTH, SSM_GROUPS, SSM_GROUP, SSM_STATE), SSM_STATE ** -0.5),
        'ssm_c_im': nrm(29, (DEPTH, SSM_GROUPS, SSM_GROUP, SSM_STATE), SSM_STATE ** -0.5),
        'ssm_d': nrm(30, (DEPTH, SSM_GROUPS, SSM_GROUP), 0.5),
        'w_a': nrm(31, (DEPTH, Q_W, D_MODEL), Q_W ** -0.5),
        'w_glu1': nrm(32, (DEPTH, SSM_WIDTH, D_MODEL), SSM_WIDTH ** -0.5),
        'w_glu2': nrm(33, (DEPTH, SSM_WIDTH, D_MODEL), SSM_WIDTH ** -0.5),
        'w_o': nrm(34, (DEPTH, D_MODEL, D_MODEL), D_MODEL ** -0.5),
        'g_ffn': gain(35, (DEPTH, D_MODEL)),
        'w_up': nrm(36, (DEPTH, D_MODEL, 2 * D_FF), D_MODEL ** -0.5),
        'conv_w': nrm(37, (DEPTH, CONV_W, D_FF), CONV_W ** -0.5),
        'conv_b': nrm(38, (DEPTH, D_FF), 0.02),
        'w_down': nrm(39, (DEPTH, D_FF, D_MODEL), D_FF ** -0.5),
        'g_ple': gain(40, (DEPTH, D_MODEL)),
        'w_ple_gate': nrm(41, (DEPTH, D_MODEL, D_MODEL), D_MODEL ** -0.5),
        'w_ple': nrm(42, (DEPTH, PLE_DIM, D_MODEL), PLE_DIM ** -0.5),
    }

def reference(x_prompt, x_sample, cache_cmp, cache_sel, cache_win, state_ssm_re, state_ssm_im, state_conv,
              page_table, p_prompt, p_sample, g_attn, w_in, g_q, g_kc, g_ks, g_kw,
              cmp_wk1, cmp_pek, cmp_wk2, cmp_wv1, cmp_pev, cmp_wv2,
              ssm_a_re, ssm_a_im, ssm_log_dt, ssm_b_re, ssm_b_im, ssm_c_re, ssm_c_im, ssm_d,
              w_a, w_glu1, w_glu2, w_o, g_ffn, w_up, conv_w, conv_b, w_down, g_ple, w_ple_gate, w_ple):
    Bp, Tp = x_prompt.shape[:2]
    Ts = x_sample.shape[1]
    past = page_table.shape[1] * PAGE_SIZE
    pos_p = jnp.arange(Tp)
    pos_s = past + jnp.arange(Ts)
    zeros_h = jnp.zeros((Bp, SSM_GROUPS, SSM_STATE), x_prompt.dtype)
    zeros_c = jnp.zeros((Bp, CONV_W - 1, D_FF), x_prompt.dtype)
    layer_w = (g_attn, w_in, g_q, g_kc, g_ks, g_kw, cmp_wk1, cmp_pek, cmp_wk2, cmp_wv1, cmp_pev, cmp_wv2,
               ssm_a_re, ssm_a_im, ssm_log_dt, ssm_b_re, ssm_b_im, ssm_c_re, ssm_c_im, ssm_d,
               w_a, w_glu1, w_glu2, w_o, g_ffn, w_up, conv_w, conv_b, w_down, g_ple, w_ple_gate, w_ple)
    st = [[] for _ in range(12)]
    hp, hs = x_prompt, x_sample
    for i in range(DEPTH):
        lw = [w[i] for w in layer_w]
        hp, rows, hr, hi, cv = block(hp, p_prompt[i], pos_p, lw, nsa_prompt, zeros_h, zeros_h, zeros_c)
        for j, a in enumerate(list(rows) + [hr, hi, cv]):
            st[j].append(a)
        nsa_s = functools.partial(nsa_sample, cmp_pool=cache_cmp[i], sel_pool=cache_sel[i],
                                  win_buf=cache_win[i], page_table=page_table)
        hs, rows, hr, hi, cv = block(hs, p_sample[i], pos_s, lw, nsa_s, state_ssm_re[i], state_ssm_im[i], state_conv[i])
        for j, a in enumerate(list(rows) + [hr, hi, cv]):
            st[6 + j].append(a)
    return (hp, hs,
            jnp.stack(st[0]), jnp.stack(st[1]), jnp.stack(st[2]), jnp.stack(st[3]), jnp.stack(st[4]), jnp.stack(st[5]),
            jnp.stack(st[6]), jnp.stack(st[7]), jnp.stack(st[8]), jnp.stack(st[9]), jnp.stack(st[10]), jnp.stack(st[11]))


_drawn_inputs = setup_inputs


def setup_inputs(seed=0):
    import zlib

    import numpy as np

    out = dict(_drawn_inputs(seed))
    spreads = {}
    factors = {'g_q': 8.0, 'cmp_pek': 8.0, 'ssm_a_re': 4.22, 'conv_b': 4.26, 'g_ple': 5.043}
    for name, (base, spread) in spreads.items():
        noise = np.random.default_rng([zlib.crc32(name.encode()), seed]).standard_normal(out[name].shape)
        drawn = base * np.exp(spread * noise) if base else spread * noise
        out[name] = jnp.asarray(drawn.astype(out[name].dtype))
    for name, factor in factors.items():
        out[name] = (out[name] * factor).astype(out[name].dtype)
    return out
```

```python
from contextlib import ExitStack

import concourse.bass as bass
from concourse import mybir

F32 = mybir.dt.float32
I32 = mybir.dt.int32
ALU = mybir.AluOpType
ACT = mybir.ActivationFunctionType
AX = mybir.AxisListType.X
ds = bass.ds

P = 128
D, DEPTH, SEQ, NB = 1024, 2, 256, 8
NT = SEQ + NB
KD = D // P
H, KV, HD = 8, 2, 64
QW, KVW = H * HD, KV * HD
PAGE, PAGES = 128, 2
PAST = PAGE * PAGES
CB, CS, NCMP = 32, 16, (SEQ - 32) // 16 + 1
SSMW, GC, NG, NS_ = 512, 16, 32, 64
ST = NG * NS_ // P
FF = 2816
KF = FF // P
PLE = 256
NIN = QW + 6 * KVW + 3 * H + SSMW + 2 * D
QKV = QW + 6 * KVW + 3 * H
U0, GA0 = QKV, QKV + SSMW
EPS = 1e-6
SCALE = HD ** -0.5
NEG = -1e30
NSEQ = NB + 1
KEYS = 2 * (PAST + 1) + NCMP
NEW0, CMP0 = 2 * PAST, 2 * PAST + 2
XR = 2 * NSEQ + 1
INV2PI = 0.15915494309189535
CONSTS = 17
ROUND = 12582912.0
PI2_A, PI2_B, PI2_C = 6.28125, 0.0019350051879882812, 3.0199157663446332e-07

SLOT = 2240
SLOTS = 5
QW_CHUNKS = [(256 * i, 256) for i in range(4)] + [(1024, 280)]

ACT_PRO, DVE_PRO = 4, 4
BANKS = 3

def offsets(stages):
    at, out = 0, {}
    for name, n in stages:
        out[name] = at
        at += n
    return out, at


A_AT, ACT_LAYER = offsets((
    ("caches", 2 * NB), ("pe", 1), ("qkv", 3 * len(QW_CHUNKS)), ("u", 4), ("turn_qk", 5), ("cmp", 1), ("hidden", 2),
    ("v_cmp", 3), ("s_probs", 1), ("p_probs", 2 * H + 4), ("gates", 2 * KD), ("states", 1), ("glu", KD), ("conv", 1),
    ("up", KF), ("gate_rows", 6), ("ple_in", 2), ("ple", KD), ("ple_gate", KD)))
V_AT, DVE_LAYER = offsets((
    ("params", 1), ("h0", 1), ("norm0", 1), ("c", 2), ("b", 2), ("s_gates", 1), ("k_cmp", 1), ("s_scores", 2),
    ("c_scores", 2), ("p_scores", 2 * H), ("s_drive", 1), ("drive", ST), ("w_a", KD), ("glu", KD), ("w_o", KD),
    ("norm1", 1), ("up", KF), ("down", KD), ("norm2", 1)))


def act_jobs(L, stage, n=0):
    return L * ACT_LAYER + (ACT_PRO + A_AT[stage] + n)


def dve_jobs(L, stage, n=0):
    return L * DVE_LAYER + (DVE_PRO + V_AT[stage] + n)


def probs_turned(L, u):
    return act_jobs(L, "p_probs", u + u // 4 + 2)


def weight_chunks():
    names = [("qkv", i) for i in range(5)]
    names += [("u", i) for i in range(2)]
    names += [("cmp", i) for i in range(2)]
    names += [("gate", i) for i in range(8)]
    names += [("w_a", i) for i in range(2)]
    names += [("glu", i) for i in range(4)]
    names += [("w_o", i) for i in range(4)]
    names += [("up", i) for i in range(22)]
    names += [("down", i) for i in range(16)]
    names += [("ple", 0)]
    names += [("ple_gate", i) for i in range(4)]
    return names


CHUNKS = weight_chunks()
NCH = len(CHUNKS)
assert NCH % SLOTS == 0


def trunk(nc, A, C, O):
    ctx = ExitStack()
    with ctx:
        def sb(name, shape, dt=F32):
            return ctx.enter_context(nc.sbuf_tensor(name, shape, dt))

        def sem(name):
            return ctx.enter_context(nc.semaphore(name))

        ring = sb("ring", [P, SLOTS, SLOT])
        hT = sb("hT", [P, KD, NT])
        xn = sb("xn", [P, KD, NT])
        z = sb("z", [P, 3, QKV])
        vpast = sb("vpast", [P, NB, 2, PAGES, KVW])
        prompt_cmp = sb("prompt_cmp", [P, 4 * KVW])
        R1 = sb("R1", [P, KF * NT])
        kall = sb("kall", [P, NB * KEYS])
        sg = sb("sg", [P, 2, KD, NT])
        kT = sb("kT", [P, 2, SEQ])
        qpad = sb("qpad", [P, NB * 64 + 64])
        S = sb("S", [P, 2, 2, SEQ])
        PT = sb("PT", [P, 2, 2, 2, SEQ])
        pcT = sb("pcT", [NCMP, 2, 512])
        aT = sb("aT", [P, 4, NT])
        uT = sb("uT", [P, 4, NT])
        upad = sb("upad", [P, 4, 4, NB])
        BT = sb("BT", [P, 2, 4, P])
        CT = sb("CT", [P, 2, 4, P])
        prm_rows = sb("prm_rows", [28, P])
        ssm_rows = sb("ssm_rows", [ST, 3, P])
        dt_rows = sb("dt_rows", [ST, 2])
        h0_rows = sb("h0_rows", [P, 2, P])
        prm = sb("prm", [P, 28 + 3 * ST])
        gains = sb("gains", [P, 4, HD])
        w2 = sb("w2", [P, 3, HD])
        pe_rows = sb("pe_rows", [16, 2, P])
        pe_col = sb("pe_col", [P, 2])
        rstd = sb("rstd", [P, NT])
        ss = sb("ss", [P, 3, 14])
        cs = sb("cs", [P, 2, 8, ST])
        sm = sb("sm", [P, 16, ST])
        h0 = sb("h0", [P, 2, NB * ST])
        hs = sb("hs", [P, 2, NB * ST])
        hfin = sb("hfin", [P, 2, ST])
        kcmp = sb("kcmp", [P, NCMP])
        mx = sb("mx", [P, 2, 4])
        sums = sb("sums", [P, 2, 4])
        cmx = sb("cmx", [P, 16])
        csum = sb("csum", [P, 16])
        bg = sb("bg", [P, 3, 24])
        snew = sb("snew", [64, 2, NB])
        sq4 = sb("sq4", [64, 16])
        gg = sb("gg", [64, 3])
        g64 = sb("g64", [64, 8, 3])
        GX = sb("GX", [P, 2, 2 + NT])
        pt_sb = sb("pt_sb", [1, NB * PAGES], I32)
        c_id = sb("c_id", [P, P])
        c_mask = sb("c_mask", [P, SEQ])
        c_cos = sb("c_cos", [P, 3, HD])
        c_sin = sb("c_sin", [P, 3, HD])
        c_ccos = sb("c_ccos", [P, NCMP])
        c_csin = sb("c_csin", [P, NCMP])
        c_cmask = sb("c_cmask", [P, 2, 2, NCMP])
        c_ones = sb("c_ones", [P, P])
        c_gmask = sb("c_gmask", [P, 2])
        c_rmask = sb("c_rmask", [P, 2])
        c_qmask = sb("c_qmask", [P, 4])
        c_pow = sb("c_pow", [P, 8])
        c_sel = sb("c_sel", [NB, 64])
        c_diag = sb("c_diag", [64, NB])
        c_head = sb("c_head", [64, 8])
        c_bias = sb("c_bias", [P, 2])

        xrows = R1[:, 0:3 * D].rearrange("p (t d) -> p t d", t=3)
        XT = R1[:, 0:2 * XR * P].rearrange("p (v r t) -> p v r t", v=2, r=XR)
        rot = R1[:, 0:2048].rearrange("p (b c i t) -> p b c i t", b=2, c=2, i=2)
        rotw = R1[:, 2048:3072].rearrange("p (w c i t) -> p w c i t", w=2, c=2, i=2)
        W1 = R1[:, 3072:3584].rearrange("p (c t) -> p c t", c=2)
        W2 = R1[:, 3584:4096].rearrange("p (c t) -> p c t", c=2)
        G = R1[:, 4096:4608].rearrange("p (c t) -> p c t", c=2)
        HH = R1[:, 4608:5632].rearrange("p (b c t) -> p b c t", b=2, c=2)
        act = R1[:, 0:KF * NT].rearrange("p (f t) -> p f t", f=KF)
        keys = kall[:].rearrange("p (s k) -> p s k", s=NB)
        conv_rows = kall[0:20, 0:FF]
        gp_rows = kall[0:10, 0:FF]
        sgf = sg[:].rearrange("p g k t -> p (g k t)")
        bst = sgf[:, 0:512].rearrange("p (r i c) -> p r i c", r=2, i=ST)
        bpad = sgf[:, 512:1536].rearrange("p (r i g c) -> p r i g c", r=2, i=ST, g=2)
        bw = sgf[:, 1536:2560].rearrange("p (w i c) -> p w i c", w=4, i=ST)
        cst_c = sgf[:, 2560:3072].rearrange("p (r k s) -> p r k s", r=2, k=4)
        cpad = sgf[:, 3072:4096].rearrange("p (r k g s) -> p r k g s", r=2, k=4, g=2)
        yT = z[:, 0, 0:4 * NT].rearrange("p (c t) -> p c t", c=4)
        pT = z[:, 1, 0:2 * NT].rearrange("p (k t) -> p k t", k=2)
        p_rows = z[:, 2, 0:3 * PLE].rearrange("p (t k) -> p t k", t=3)
        plT = sg[:, 0]
        qT = aT[:, :, 0:SEQ]
        Sf = S[:].rearrange("p a b k -> p (a b k)")
        ang = Sf[:, 0:24 * ST].rearrange("p (w k i) -> p w k i", w=3, k=8)
        hg = Sf[:, 0:4 * NSEQ * NCMP].rearrange("p (v n) -> p v n", v=2)
        PTf = PT[:].rearrange("p a b c q -> p (a b c q)")
        kst = PTf[:, 0:1024].rearrange("p (b v g k) -> p b v g k", b=2, v=2, g=PAGES)
        cst = PTf[:, 1024:2048].rearrange("p (b x) -> p b x", b=2)
        SS = R1[0:64, 3072:3072 + KEYS]
        PTs = R1[:, 3632:4080]
        SP_ = R1[:, 4080:4320].rearrange("p (h n) -> p h n", h=16)
        vcmp = R1[0:NCMP, 4320:5472].rearrange("p (s k) -> p s k", s=NSEQ)
        kct = R1[:, 5472:5742].rearrange("p (r n) -> p r n", r=2)
        st_out = h0_rows
        fin_out = ssm_rows[:, 0:2, :]
        tg = PTf[:, 0:2 * NT].rearrange("p (b t) -> p b t", b=2)
        cv = PTf[:, 2 * NT:4 * NT].rearrange("p (b t) -> p b t", b=2)
        gcol = PTf[:, 4 * NT:4 * NT + 10 * KF].rearrange("p (f t) -> p f t", f=KF)
        cvT = PTf[:, 4 * NT + 10 * KF:4 * NT + 30 * KF].rearrange("p (f t) -> p f t", f=KF)
        ident = c_id[:]

        bankA = [ctx.enter_context(nc.psum_tensor(f"bank_act{i}", [P, 512], F32)) for i in range(BANKS)]
        bankV = [ctx.enter_context(nc.psum_tensor(f"bank_dve{i}", [P, 512], F32)) for i in range(BANKS)]
        bankO = ctx.enter_context(nc.psum_tensor("bank_o", [P, 512], F32))
        bankY = ctx.enter_context(nc.psum_tensor("bank_y", [P, 512], F32))

        consts_in = sem("consts_in")
        x_in = sem("x_in")
        weights_in = [sem(f"weights_in{i}") for i in range(SLOTS)]
        weights_used = sem("weights_used")
        act_ready, act_freed = sem("act_ready"), sem("act_freed")
        dve_ready, dve_freed = sem("dve_ready"), sem("dve_freed")
        act_step, dve_step, pool_step = sem("act_step"), sem("dve_step"), sem("pool_step")
        params_in = sem("params_in")
        smat_in = sem("smat_in")
        h0_in = sem("h0_in")
        k_in = [sem("k_in0"), sem("k_in1")]
        v_in = sem("v_in")
        cmp_in = [sem(f"cmp_in{i}") for i in range(3)]
        rows_out = sem("rows_out")
        rows_back = sem("rows_back")
        pe_in = sem("pe_in")
        conv_in = sem("conv_in")
        ple_in = sem("ple_in")
        states_out, conv_out, y_out = sem("states_out"), sem("conv_out"), sem("y_out")
        copies_out = sem("copies_out")
        squared = sem("squared")
        var_ready, std_ready = sem("var_ready"), sem("std_ready")
        normed = sem("normed")
        dt_rows_ready = sem("dt_rows_ready")
        dt_ready, decay_exp, trig_arg, trig_ready = (sem("dt_ready"), sem("decay_exp"), sem("trig_arg"),
                                                      sem("trig_ready"))
        decay_ready = sem("decay_ready")
        b_ready, c_ready = sem("b_ready"), sem("c_ready")
        rot_ready, rot_used = sem("rot_ready"), sem("rot_used")
        zeroed = sem("zeroed")
        gates_tanh, gates_ready = sem("gates_tanh"), sem("gates_ready")
        heads_sq = sem("heads_sq")
        hvar_ready, hstd_ready = sem("hvar_ready"), sem("hstd_ready")
        roped, u_spread = sem("roped"), sem("u_spread")
        pe_bias, hidden = sem("pe_bias"), sem("hidden")
        kcmp_ready = sem("kcmp_ready")
        s_max, s_exp, s_prob = sem("s_max"), sem("s_exp"), sem("s_prob")
        c_arg, c_exp, c_prob = sem("c_arg"), sem("c_exp"), sem("c_prob")
        p_max, p_exp, p_prob = sem("p_max"), sem("p_exp"), sem("p_prob")
        p_turned = sem("p_turned")
        o_ready, o_taken = sem("o_ready"), sem("o_taken")
        state_ready, y_used = sem("state_ready"), sem("y_used")
        y_ready, y_taken, y_gelu = sem("y_ready"), sem("y_taken"), sem("y_gelu")
        glu_tanh, glu_done = sem("glu_tanh"), sem("glu_done")
        merged = sem("merged")
        h_mixed, h_ffn, h_done = sem("h_mixed"), sem("h_ffn"), sem("h_done")
        gate_copied, conved, ff_gelu, ff_done = (sem("gate_copied"), sem("conved"), sem("ff_gelu"),
                                                 sem("ff_done"))
        ple_tanh, ple_gate_used = sem("ple_tanh"), sem("ple_gate_used")
        rows_done = sem("rows_done")

        block = ctx.enter_context(nc.Block())
        (y_prompt, y_sample, cmp_p, sel_p, win_p, re_p, im_p, conv_p,
         cmp_s, sel_s, win_s, re_s, im_s, conv_s) = O

        @block.sync
        def _(sp):
            def cols(name, k0, nk, c0, n):
                w = A[name].rearrange("l (k p) n -> p (l k) n", p=P)
                per = A[name].shape[1] // P
                return lambda L: w[:, ds(L * per + k0, nk), c0:c0 + n]

            def heads(name, c0, n, half):
                w = A[name].rearrange("l (g c d) n -> d (l g) c n", g=KV, c=4)
                return lambda L: w[:, ds(L * KV + half, 1), :, c0:c0 + n]

            with sp.Fori(0, DEPTH) as L:
                for m, (name, i) in enumerate(CHUNKS):
                    slot = m % SLOTS
                    sp.wait_ge(weights_used, L * NCH + (m + 2))

                    def put(k, n, off, width, src, rows=slice(0, P)):
                        dst = ring[rows, slot, 0:k * width].rearrange("p (k n) -> p k n", k=k)
                        sp.dma_start(dst[:, :, off:off + n], src).then_inc(weights_in[slot], 16)

                    if name == "cmp":
                        w = A[("cmp_wk1", "cmp_wv1")[i]].rearrange("l (j a) d f -> (a d) (l j) f", a=2)
                        for j in (0, 8):
                            sp.dma_start(ring[:, slot, j * P:(j + 8) * P].rearrange("p (j n) -> p j n", j=8),
                                         w[:, ds(L * 16 + j, 8), :]).then_inc(weights_in[slot], 16)
                    elif name == "qkv":
                        c0, n = QW_CHUNKS[i]
                        put(KD, n, 0, n, cols("w_in", 0, KD, c0, n)(L))
                    elif name == "u":
                        put(KD, 256, 0, 256, cols("w_in", 0, KD, U0 + 256 * i, 256)(L))
                    elif name == "gate":
                        put(KD, 256, 0, 256, cols("w_in", 0, KD, GA0 + 256 * i, 256)(L))
                    elif name == "w_a":
                        for g in range(KV):
                            w = A["w_a"].rearrange("l (g c d) n -> d (l g) c n", g=KV, c=4)
                            put(4, 512, 0, 512, w[:, ds(L * KV + g, 1), :, 512 * i:512 * i + 512]
                                .rearrange("d a c n -> d (a c) n"), slice(64 * g, 64 * g + 64))
                    elif name == "glu":
                        put(4, 256, 0, 512, cols("w_glu1", 0, 4, 256 * i, 256)(L))
                        put(4, 256, 256, 512, cols("w_glu2", 0, 4, 256 * i, 256)(L))
                    elif name == "w_o":
                        put(KD, 256, 0, 256, cols("w_o", 0, KD, 256 * i, 256)(L))
                    elif name == "up":
                        put(KD, P, 0, 256, cols("w_up", 0, KD, P * i, P)(L))
                        put(KD, P, P, 256, cols("w_up", 0, KD, FF + P * i, P)(L))
                    elif name == "down":
                        put(11, P, 0, P, cols("w_down", 11 * (i % 2), 11, P * (i // 2), P)(L))
                    elif name == "ple":
                        put(2, D, 0, D, cols("w_ple", 0, 2, 0, D)(L))
                    elif name == "ple_gate":
                        put(KD, 256, 0, 256, cols("w_ple_gate", 0, KD, 256 * i, 256)(L))

        def dmas_of(name):
            return 2 if name in ("cmp", "w_a", "glu", "up") else 1

        slot_total = [sum(16 * dmas_of(n) for n, _ in CHUNKS[s::SLOTS]) for s in range(SLOTS)]

        def slot_count(m):
            return sum(16 * dmas_of(n) for n, _ in CHUNKS[m % SLOTS:m + 1:SLOTS])

        @block.gpsimd
        def _(pool):
            def await_(what, count):
                count = pool.to_reg(count)
                pool.wait_ge(consts_in, 16 * CONSTS)
                pool.wait_ge(what, count)

            with nc.allow_non_contiguous_dma(reason="short rows"):
                for t, name in ((c_id, "ident"), (c_mask, "mask"), (c_cos, "cos"), (c_sin, "sin"),
                                (c_ccos, "ccos"), (c_csin, "csin"), (c_cmask, "cmask"), (c_ones, "ones"),
                                (c_gmask, "gmask"), (c_rmask, "rmask"), (c_qmask, "qmask"), (c_pow, "pow"), (c_sel, "sel"),
                                (c_diag, "diag"), (c_head, "head"), (c_bias, "bias")):
                    pool.dma_start(t[:], C[name]).then_inc(consts_in, 16)
                pool.dma_start(pt_sb[:], A["page_table"].rearrange("s (a g) -> a (s g)", a=1)).then_inc(consts_in, 16)
                pool.dma_start(xrows[:, 0:2, :], A["x_prompt"].rearrange("b (t p) d -> p (b t) d", p=P)).then_inc(x_in, 16)
                pool.dma_start(xrows[0:NB, 2, :], A["x_sample"].rearrange("s a d -> s (a d)")).then_inc(x_in, 16)
                pool.memset(qpad[:], 0.0).then_inc(zeroed, 1)
                pool.memset(GX[:, :, 0:2], 0.0).then_inc(zeroed, 1)
                pool.wait_ge(consts_in, 16 * CONSTS)
                with pool.Fori(0, DEPTH) as L:
                    pool.sem_clear(pool_step)
                    step = [0]

                    def link(ins):
                        step[0] += 1
                        ins.then_inc(pool_step, 1)
                        pool.wait_ge(pool_step, step[0])

                    def load(dst, src, done):
                        pool.dma_start(dst, src).then_inc(done, 16)

                    def layer(name, how, **kw):
                        return A[name].rearrange(how, **kw)

                    await_(h_done, L * KD + 1)
                    for j, g in enumerate(("g_attn", "g_ffn", "g_ple")):
                        load(prm_rows[KD * j:KD * j + KD, :], A[g].rearrange("l (k p) -> (l k) p", p=P)[ds(L * KD, KD), :], params_in)
                    load(prm_rows[24:28, :], A["ssm_d"].rearrange("l (k g) c -> (l k) (g c)", g=8)[ds(L * 4, 4), :], params_in)
                    load(ssm_rows[:, 0, :], A["ssm_a_re"].rearrange("l (i g) s -> (l i) (g s)", g=2)[ds(L * ST, ST), :], params_in)
                    load(ssm_rows[:, 1, :], A["ssm_a_im"].rearrange("l (i g) s -> (l i) (g s)", g=2)[ds(L * ST, ST), :], params_in)
                    load(dt_rows[:], A["ssm_log_dt"].rearrange("l (i g) -> (l i) g", g=2)[ds(L * ST, ST), :], params_in)
                    for j, g in enumerate(("g_q", "g_kc", "g_ks", "g_kw")):
                        load(gains[:, j, :], A[g][ds(L, 1), :].broadcast_to([P, HD]), params_in)
                    load(w2[:, 0, :], A["cmp_wk2"].rearrange("l f d -> (l f) d")[ds(L * P, P), :], params_in)
                    load(w2[:, 1, 0:32], A["cmp_wk2"].rearrange("l f d -> (l f) d")[ds(L * P, P), 32:64], params_in)
                    load(w2[:, 1, 32:64], A["cmp_wk2"].rearrange("l f d -> (l f) d")[ds(L * P, P), 0:32], params_in)
                    load(w2[:, 2, :], A["cmp_wv2"].rearrange("l f d -> (l f) d")[ds(L * P, P), :], params_in)
                    load(pe_rows[:, 0, :], A["cmp_pek"].rearrange("l (j a) d -> (l j) (a d)", a=2)[ds(L * 16, 16), :], pe_in)
                    load(pe_rows[:, 1, :], A["cmp_pev"].rearrange("l (j a) d -> (l j) (a d)", a=2)[ds(L * 16, 16), :], pe_in)
                    load(h0_rows[:, 0, :], A["state_ssm_re"].rearrange("l s (i g) n -> (l s i) (g n)", g=2)[ds(L * P, P), :], h0_in)
                    load(h0_rows[:, 1, :], A["state_ssm_im"].rearrange("l s (i g) n -> (l s i) (g n)", g=2)[ds(L * P, P), :], h0_in)

                    sel_pool = A["cache_sel"].rearrange("l n t v g d -> t (l n) v (g d)")
                    cmp_pool = A["cache_cmp"].rearrange("l n (t a) v g d -> t (l n) a (v g) d", a=2)
                    win = A["cache_win"].rearrange("l s (b t) v g d -> t (l s) b v (g d)", b=PAGES)
                    n_pool = A["cache_sel"].shape[1]
                    for s in range(NB):
                        await_(act_freed, act_jobs(L, "caches", 2 * (s - 2) + 2 if s >= 2 else 0))
                        for b in range(PAGES):
                            page = pool.value_load(pt_sb[0:1, s * PAGES + b:s * PAGES + b + 1], min_val=0, max_val=n_pool - 1)
                            load(kst[:, s % 2, 0, b, :], sel_pool[:, ds(L * n_pool + page, 1), 0, :].rearrange("t a k -> t (a k)"), k_in[s % 2])
                            load(vpast[:, s, 0, b, :], sel_pool[:, ds(L * n_pool + page, 1), 1, :].rearrange("t a k -> t (a k)"), v_in)
                            for a in range(2):
                                load(cst[64 * b:64 * b + 64, s % 2, :].rearrange("p (w a d) -> p w a d", w=4, a=2)[:, :, a, :],
                                     cmp_pool[:, ds(L * n_pool + page, 1), a, :, :].rearrange("t l w d -> t (l w) d"), cmp_in[s % 2])
                        load(kst[:, s % 2, 1, :, :], win[:, ds(L * NB + s, 1), :, 0, :].rearrange("t a b k -> t (a b) k"), k_in[s % 2])
                        load(vpast[:, s, 1, :, :], win[:, ds(L * NB + s, 1), :, 1, :].rearrange("t a b k -> t (a b) k"), v_in)

                    load(bst[:, 0], A["ssm_b_re"].rearrange("l (i g) s c -> (g s) (l i) c", g=2)[:, ds(L * ST, ST), :], smat_in)
                    load(bst[:, 1], A["ssm_b_im"].rearrange("l (i g) s c -> (g s) (l i) c", g=2)[:, ds(L * ST, ST), :], smat_in)
                    load(cst_c[:, 0], A["ssm_c_re"].rearrange("l (k g) c s -> (g c) (l k) s", g=8)[:, ds(L * 4, 4), :], smat_in)
                    load(cst_c[:, 1], A["ssm_c_im"].rearrange("l (k g) c s -> (g c) (l k) s", g=8)[:, ds(L * 4, 4), :], smat_in)

                    pool.dma_start(win_s.rearrange("l s t v g d -> (l s) (t v g d)")[ds(L * NB, NB), 0:(PAST - 1) * 256],
                                   A["cache_win"].rearrange("l s t v g d -> (l s) (t v g d)")[ds(L * NB, NB), 256:PAST * 256]).then_inc(copies_out, 16)
                    pool.dma_start(conv_s.rearrange("l s j f -> (l s) j f")[ds(L * NB, NB), 0, :],
                                   A["state_conv"].rearrange("l s j f -> (l s) j f")[ds(L * NB, NB), 1, :]).then_inc(copies_out, 16)

                    await_(roped, L * 3 + 3)
                    for j, (outp, outs) in enumerate(((cmp_p, cmp_s), (sel_p, sel_s), (win_p, None))):
                        c0 = QW + 2 * KVW * j
                        pool.dma_start(outp.rearrange("l b (t p) v g d -> p (l b t) (v g d)", p=P)[:, ds(L * 2, 2), :],
                                       z[:, 0:2, c0:c0 + 256]).then_inc(rows_out, 16)
                        if outs is not None:
                            pool.dma_start(outs.rearrange("l s a v g d -> (l s) (a v g d)")[ds(L * NB, NB), :],
                                           z[0:NB, 2, c0:c0 + 256]).then_inc(rows_out, 16)
                    pool.dma_start(win_s.rearrange("l s t v g d -> (l s) (t v g d)")[ds(L * NB, NB), (PAST - 1) * 256:PAST * 256],
                                   z[0:NB, 2, 1024:1280]).then_inc(rows_out, 16)
                    await_(rows_out, L * 96 + 96)
                    for a in range(2):
                        load(prompt_cmp[:].rearrange("p (w a d) -> p w a d", w=4, a=2)[:, :, a, :],
                             cmp_p.rearrange("l b (t a) v g d -> (l b t) a (v g) d", a=2)[ds(L * P, P), a, :, :], rows_back)

                    await_(trig_ready, L + 1)
                    for q in range(ST // 2):
                        if q == 0:
                            await_(kcmp_ready, L + 1)
                        if q >= 2:
                            await_(rot_used, L * (ST // 2) + (q - 1))
                        T = rot[:, q % 2]
                        link(pool.memset(T[:, 0, :, 0:1], 1.0))
                        link(pool.memset(T[:, 1, :, 0:1], 0.0))
                        for k in range(8):
                            n = 1 << k
                            cc = cs[:, 0, k, 2 * q:2 * q + 2].unsqueeze(1).unsqueeze(3).broadcast_to([P, 2, 2, n])
                            sn = cs[:, 1, k, 2 * q:2 * q + 2].unsqueeze(1).unsqueeze(3).broadcast_to([P, 2, 2, n])
                            pool.tensor_tensor(rotw[:, 0, :, :, 0:n], T[:, :, :, 0:n], cc, ALU.mult)
                            link(pool.tensor_tensor(rotw[:, 1, :, :, 0:n], T[:, :, :, 0:n], sn, ALU.mult))
                            last = pool.tensor_tensor(T[:, 0, :, n:2 * n], rotw[:, 0, 0, :, 0:n], rotw[:, 1, 1, :, 0:n], ALU.subtract)
                            last = pool.tensor_tensor(T[:, 1, :, n:2 * n], rotw[:, 0, 1, :, 0:n], rotw[:, 1, 0, :, 0:n], ALU.add)
                            if k < 7:
                                link(last)
                            else:
                                last.then_inc(rot_ready, 1)

                    await_(o_ready, L * 5 + 1)
                    load(conv_rows[0:16, :], A["state_conv"].rearrange("l s j f -> (l s j) f")[ds(L * 16, 16), :], conv_in)
                    load(conv_rows[16:19, :], A["conv_w"].rearrange("l j f -> (l j) f")[ds(L * 3, 3), :], conv_in)
                    load(conv_rows[19:20, :], A["conv_b"][ds(L, 1), :], conv_in)
                    await_(act_freed, act_jobs(L, "states", 1))
                    for j, (o_p, o_s) in enumerate(((re_p, re_s), (im_p, im_s))):
                        pool.dma_start(o_s.rearrange("l s (i g) n -> (l s i) (g n)", g=2)[ds(L * P, P), :], st_out[:, j, :]).then_inc(states_out, 16)
                        pool.dma_start(o_p.rearrange("l b (i g) n -> (l b i) (g n)", g=2)[ds(L * ST, ST), :], fin_out[:, j, :]).then_inc(states_out, 16)
                    await_(dve_freed, dve_jobs(L, "w_o", 1))
                    load(p_rows[:, 0:2, :], A["p_prompt"].rearrange("l b (t p) k -> p (l b t) k", p=P)[:, ds(L * 2, 2), :], ple_in)
                    load(p_rows[0:NB, 2, :], A["p_sample"].rearrange("l s a k -> (l s) (a k)")[ds(L * NB, NB), :], ple_in)
                    await_(act_freed, act_jobs(L, "gate_rows", 6))
                    pool.dma_start(conv_p.rearrange("l b j f -> (l b j) f")[ds(L * 2, 2), :], gp_rows[0:2, :]).then_inc(conv_out, 16)
                    pool.dma_start(conv_s.rearrange("l s j f -> (l s) j f")[ds(L * NB, NB), 1, :], gp_rows[2:10, :]).then_inc(conv_out, 16)
                    await_(conv_out, L * 32 + 32)
                    await_(states_out, L * 64 + 64)
                await_(act_freed, act_jobs(DEPTH, "caches", 3))
                await_(dve_freed, dve_jobs(DEPTH, "params", 3))
                pool.dma_start(y_prompt.rearrange("b (t p) d -> p (b t) d", p=P), xrows[:, 0:2, :]).then_inc(y_out, 16)
                pool.dma_start(y_sample.rearrange("s a d -> s (a d)"), xrows[0:NB, 2, :]).then_inc(y_out, 16)
                pool.wait_ge(copies_out, DEPTH * 32)
                await_(rows_out, DEPTH * 96)
                await_(states_out, DEPTH * 64)
                await_(conv_out, DEPTH * 32)
                pool.wait_ge(y_out, 32)

        @block.tensor
        def _(pe):
            def small():
                pe.wait_ge(consts_in, 16 * CONSTS)

            def run(L, program, base_a, base_v):
                n_a, n_v, chunk = [0], [0], [0]

                def act_bank(few_rows=False):
                    n = n_a[0]
                    n_a[0] += 1
                    if n >= BANKS or base_a is not None:
                        count = (base_a if base_a is not None else 0) + (n - BANKS + 1 if n >= BANKS else 0)
                        if few_rows:
                            count = pe.to_reg(count)
                            small()
                        pe.wait_ge(act_freed, count)
                    return bankA[n % BANKS]

                def dve_bank(few_rows=False):
                    n = n_v[0]
                    n_v[0] += 1
                    if n >= BANKS or base_v is not None:
                        count = (base_v if base_v is not None else 0) + (n - BANKS + 1 if n >= BANKS else 0)
                        if few_rows:
                            count = pe.to_reg(count)
                            small()
                        pe.wait_ge(dve_freed, count)
                    return bankV[n % BANKS]

                def next_chunk():
                    m = chunk[0]
                    chunk[0] += 1
                    pe.wait_ge(weights_in[m % SLOTS], L * slot_total[m % SLOTS] + slot_count(m))
                    fresh[0] = True
                    return ring[:, m % SLOTS, :]

                fresh = [False]

                def mm(out, lhsT, rhs, k, nk):
                    ins = pe.matmul(out, lhsT, rhs, start=(k == 0), stop=(k == nk - 1))
                    if fresh[0]:
                        assert k < nk - 1
                        ins.then_inc(weights_used, 1)
                        fresh[0] = False
                    return ins

                program(L, act_bank, dve_bank, next_chunk, mm)
                return n_a[0], n_v[0], chunk[0]

            def prologue(L, act_bank, dve_bank, next_chunk, mm):
                pe.wait_ge(consts_in, 16 * CONSTS)
                pe.wait_ge(x_in, 32)
                for k in range(KD):
                    bank = act_bank() if k % 2 == 0 else dve_bank()
                    for t in range(2):
                        pe.transpose(bank[:, t * P:t * P + P], xrows[:, t, k * P:k * P + P], ident)
                    pe.transpose(bank[:, SEQ:NT], xrows[0:NB, 2, k * P:k * P + P], ident[0:NB, 0:NB]).then_inc(act_ready if k % 2 == 0 else dve_ready, 1)

            def layer(L, act_bank, dve_bank, next_chunk, mm):
                small()
                pe.wait_ge(params_in, L * 240 + 240)
                pe.wait_ge(dt_rows_ready, L + 1)
                bank = dve_bank(few_rows=True)
                pe.transpose(bank[:, 0:28], prm_rows[:], ident[0:28, 0:28])
                for j in range(3):
                    last = pe.transpose(bank[:, 28 + ST * j:28 + ST * j + ST], ssm_rows[:, j, :], ident[0:ST, 0:ST])
                last.then_inc(dve_ready, 1)
                pe.wait_ge(h0_in, L * 32 + 32)
                bank = dve_bank()
                for j in range(2):
                    last = pe.transpose(bank[:, P * j:P * j + P], h0_rows[:, j, :], ident)
                last.then_inc(dve_ready, 1)

                def cmp_rows(rows):
                    bank = act_bank()
                    for c in range(0, 4 * P, P):
                        last = pe.transpose(bank[:, c:c + P], rows[:, c:c + P], ident)
                    last.then_inc(act_ready, 1)

                for s in range(NB):
                    pe.wait_ge(k_in[s % 2], L * 3 * 16 * (NB // 2) + 3 * 16 * (s // 2 + 1))
                    bank = act_bank()
                    for b in range(2):
                        for g in range(PAGES):
                            c = (2 * b + g) * P
                            last = pe.transpose(bank[:, c:c + P], kst[:, s % 2, b, g, :], ident)
                    last.then_inc(act_ready, 1)
                    pe.wait_ge(cmp_in[s % 2], L * 4 * 16 * (NB // 2) + 4 * 16 * (s // 2 + 1))
                    cmp_rows(cst[:, s % 2, :])
                small()
                pe.wait_ge(pe_in, L * 32 + 32)
                bank = act_bank(few_rows=True)
                for v in range(2):
                    last = pe.transpose(bank[:, 16 * v:16 * v + 16], pe_rows[:, v, :], ident[0:16, 0:16])
                last.then_inc(act_ready, 1)

                def sum_squares(n):
                    bank = dve_bank()
                    for k in range(KD):
                        pe.wait_ge(squared, L * 3 * KD + (n * KD + k + 1))
                        last = mm(bank[:, 0:NT], c_ones[:], xn[:, k, :], k, KD)
                    last.then_inc(dve_ready, 1)

                sum_squares(0)

                pe.wait_ge(normed, L * 3 * KD + KD)
                for c0, n in QW_CHUNKS:
                    w = next_chunk()[:, 0:KD * n].rearrange("p (k n) -> p k n", k=KD)
                    for t in range(3):
                        m = P if t < 2 else NB
                        bank = act_bank()
                        for k in range(KD):
                            last = mm(bank[0:m, 0:n], xn[:, k, P * t:P * t + m], w[:, k, :], k, KD)
                        last.then_inc(act_ready, 1)

                def columns(width, tiles, rhs, nk, claim, ready):
                    w = next_chunk()[:, 0:nk * width].rearrange("p (k n) -> p k n", k=nk)
                    for j in range(tiles):
                        bank = claim()
                        for k in range(nk):
                            last = mm(bank[:, 0:NT], w[:, k, P * j:P * j + P], rhs[:, k, :], k, nk)
                        last.then_inc(ready, 1)

                for i in range(2):
                    columns(256, 2, xn, KD, act_bank, act_ready)

                pe.wait_ge(c_ready, L + 1)
                for r in range(2):
                    bank = dve_bank()
                    for k in range(4):
                        last = pe.transpose(bank[:, P * k:P * k + P], cpad[:, r, k].rearrange("p g s -> p (g s)"), ident)
                    last.then_inc(dve_ready, 1)
                pe.wait_ge(b_ready, L + 1)
                for r in range(2):
                    bank = dve_bank()
                    for k in range(4):
                        last = pe.transpose(bank[:, P * k:P * k + P], bpad[:, r, 4 * k:4 * k + 4].rearrange("p i g c -> p (i g c)"), ident)
                    last.then_inc(dve_ready, 1)

                for t in range(3):
                    small()
                    pe.wait_ge(roped, L * 3 + t + 1)
                    m = P if t < 2 else NB
                    eye = ident[0:m, 0:m]
                    bank = act_bank(few_rows=True)
                    for c in range(4):
                        last = pe.transpose(bank[:, m * c:m * c + m], z[0:m, t, KVW * c:KVW * c + KVW], eye)
                    if t < 2:
                        last.then_inc(act_ready, 1)
                        small()
                        bank = act_bank(few_rows=True)
                    off = 0 if t < 2 else 4 * NB
                    for j, c0 in enumerate((768, 1024)):
                        last = pe.transpose(bank[:, off + m * j:off + m * j + m], z[0:m, t, c0:c0 + KVW], eye)
                    last.then_inc(act_ready, 1)
                bank = dve_bank()
                pe.wait_ge(gates_ready, L + 1)
                pe.matmul(bank[0:64, 0:24], c_sel[:], bg[0:NB, 2, :], start=True, stop=True).then_inc(dve_ready, 1)

                pe.wait_ge(rows_back, L * 32 + 32)
                cmp_rows(prompt_cmp[:])
                pe.wait_ge(act_freed, act_jobs(L, "hidden"))
                for v in range(2):
                    w = next_chunk()[:, 0:16 * P].rearrange("p (j f) -> p j f", j=16)
                    bank = act_bank()
                    for j in range(16):
                        last = mm(bank[:, 0:XR * NCMP], w[:, j, :], XT[:, v, :, j:j + 8 * NCMP - 7:8], j, 16)
                    last.then_inc(act_ready, 1)
                pe.wait_ge(act_freed, act_jobs(L, "hidden", 1))
                bank = dve_bank()
                n = NSEQ * NCMP
                for r in range(2):
                    for g in range(KV):
                        last = pe.matmul(bank[64 * g:64 * g + 64, 256 * r:256 * r + n], w2[:, r, :], hg[:, 0, n * g:n * g + n],
                                         start=True, stop=True)
                last.then_inc(dve_ready, 1)
                pe.wait_ge(act_freed, act_jobs(L, "hidden", 2))
                for j in range(3):
                    bank = act_bank()
                    for i in range(3):
                        for g in range(KV):
                            c = (g * NSEQ + 3 * j + i) * NCMP
                            last = pe.matmul(bank[0:NCMP, (2 * i + g) * HD:(2 * i + g + 1) * HD], hg[:, 1, c:c + NCMP], w2[:, 2, :],
                                             start=True, stop=True)
                    last.then_inc(act_ready, 1)

                pe.wait_ge(kcmp_ready, L + 1)
                pe.wait_ge(act_freed, act_jobs(L, "v_cmp", 3))
                for c0, n in ((0, 2 * PAST), (NEW0, KEYS - NEW0)):
                    bank = dve_bank()
                    for s in range(NB):
                        last = mm(bank[0:64, 0:n], qpad[:, 64 * s:64 * s + 64], keys[:, s, c0:c0 + n], s, NB)
                    last.then_inc(dve_ready, 1)

                for g in range(KV):
                    bank = dve_bank()
                    for t in range(2):
                        for c in range(4):
                            last = pe.matmul(bank[:, NCMP * (4 * t + c):NCMP * (4 * t + c + 1)], qT[64 * g:64 * g + 64, c, P * t:P * t + P],
                                             kcmp[64 * g:64 * g + 64, :], start=True, stop=True)
                    last.then_inc(dve_ready, 1)

                def head_scores(u):
                    idx, t = divmod(u, 2)
                    c, g = divmod(idx, 2)
                    bank = dve_bank()
                    n = P * (t + 1)
                    pe.matmul(bank[:, 0:2 * n], qT[64 * g:64 * g + 64, c, P * t:P * t + P], kT[64 * g:64 * g + 64, :, 0:n],
                              start=True, stop=True).then_inc(dve_ready, 1)

                head_scores(0)

                small()
                pe.wait_ge(s_prob, L + 1)
                bank = act_bank(few_rows=True)
                for b in range(4):
                    pe.transpose(bank[:, 64 * b:64 * b + 64], SS[:, P * b:P * b + P], ident[0:64, 0:64])
                pe.transpose(bank[0:NCMP, 256:320], SS[:, CMP0:KEYS], ident[0:64, 0:64])
                for b in range(2):
                    last = pe.transpose(bank[0:NB, 320 + 64 * b:384 + 64 * b], snew[:, b, :], ident[0:64, 0:64])
                last.then_inc(act_ready, 1)
                head_scores(1)
                pe.wait_ge(v_in, L * 3 * 16 * NB + 3 * 16 * NB)
                pe.wait_ge(act_freed, act_jobs(L, "s_probs", 1))
                pe.wait_ge(o_taken, L * 5 + 1)
                for b, c0 in enumerate((896, 1152)):
                    pe.matmul(bankO[:, 0:64], z[0:NB, 2, c0:c0 + KVW], PTs[0:NB, 320 + 64 * b:384 + 64 * b],
                              start=(b == 0), stop=False, skip_group_check=True)
                for s in range(NB):
                    o = bankO[:, 8 * s:8 * s + 8]
                    for b in range(2):
                        for g in range(PAGES):
                            c = 64 * (2 * b + g) + 8 * s
                            pe.matmul(o, vpast[:, s, b, g, :], PTs[:, c:c + 8], start=False, stop=False, skip_group_check=True)
                    last = pe.matmul(o, vcmp[:, s, :], PTs[0:NCMP, 256 + 8 * s:264 + 8 * s], start=False, stop=(s == NB - 1),
                                     skip_group_check=True)
                last.then_inc(o_ready, 1)

                pe.wait_ge(c_prob, L + 1)

                def turn_cmp(c):
                    bank = act_bank()
                    for g in range(KV):
                        for t in range(2):
                            last = pe.transpose(bank[0:NCMP, (2 * g + t) * P:(2 * g + t + 1) * P], SP_[:, 8 * t + 4 * g + c, :], ident)
                    last.then_inc(act_ready, 1)

                def turn_probs(u):
                    t = u % 2
                    pe.wait_ge(p_prob, L * 16 + u + 1)
                    bank = act_bank()
                    for b in range(2):
                        for k in range(t + 1):
                            c = ((t + 1) * b + k) * P
                            last = pe.transpose(bank[:, c:c + P], S[:, u % 2, b, P * k:P * k + P], ident)
                    last.then_inc(act_ready, 1)

                def head_out(idx):
                    c, g = divmod(idx, 2)
                    pe.wait_ge(act_freed, probs_turned(L, 2 * idx + 1))
                    if g == 0:
                        pe.wait_ge(o_taken, L * 5 + 1 + c + 1)
                    o = bankO[64 * g:64 * g + 64, :]
                    vc = (896, 1152)
                    pe.matmul(o[:, 0:SEQ], vcmp[:, NB, HD * g:HD * g + HD], pcT[:, c % 2, 2 * P * g:2 * P * g + 2 * P],
                              start=True, stop=False, skip_group_check=True)
                    for b in range(2):
                        pe.matmul(o[:, 0:SEQ], z[:, 0, vc[b] + HD * g:vc[b] + HD * g + HD], PT[:, idx % 2, b, 0, :],
                                  start=False, stop=False, skip_group_check=True)
                    for b in range(2):
                        last = pe.matmul(o[:, P:SEQ], z[:, 1, vc[b] + HD * g:vc[b] + HD * g + HD], PT[:, idx % 2, b, 1, P:SEQ],
                                         start=False, stop=(b == 1), skip_group_check=True)
                    if g == 1:
                        last.then_inc(o_ready, 1)

                for u in range(2 * H):
                    if u + 2 < 2 * H:
                        head_scores(u + 2)
                    if u % 4 == 0:
                        turn_cmp(u // 4)
                    turn_probs(u)
                    if u % 2 == 0 and u >= 2:
                        head_out(u // 2 - 1)
                head_out(H - 1)

                pe.wait_ge(dve_freed, dve_jobs(L, "b", 2))
                pe.wait_ge(u_spread, L + 1)
                bank = dve_bank()
                for k in range(4):
                    for r in range(2):
                        last = pe.matmul(bank[:, P * (4 * r + k) // 4:P * (4 * r + k + 1) // 4], BT[:, r, k, :],
                                         upad[:, k].rearrange("p j s -> p (j s)"), start=True, stop=True)
                last.then_inc(dve_ready, 1)

                def drive(i):
                    a, k = 32 * (i % 4), i // 4
                    bank = dve_bank()
                    for r in range(2):
                        last = pe.matmul(bank[:, SEQ * r:SEQ * r + SEQ], BT[a:a + 32, r, k, :], uT[a:a + 32, k, 0:SEQ],
                                         start=True, stop=True)
                    last.then_inc(dve_ready, 1)

                def outputs(i):
                    a, k = 32 * (i % 4), i // 4
                    pe.wait_ge(state_ready, L * ST + i + 1)
                    if i % 4 == 0:
                        pe.wait_ge(y_taken, L * 4 + k + 1)
                    o = bankY[a:a + 32, :]
                    for r in range(2):
                        pe.matmul(o[:, 0:SEQ], CT[:, r, k, a:a + 32], HH[:, i % 2, r, :], start=(r == 0), stop=(r == 1))
                    for r in range(2):
                        last = pe.matmul(o[:, SEQ:NT], CT[:, r, k, a:a + 32], hs[:, r, i:i + ST * (NB - 1) + 1:ST],
                                         start=(r == 0), stop=(r == 1))
                    last.then_inc(y_ready, 1)

                drive(0)
                for i in range(ST):
                    if i + 1 < ST:
                        drive(i + 1)
                    if i % 2 == 0:
                        w = next_chunk()[:, 0:KD * 256].rearrange("p (k n) -> p k n", k=KD)
                    bank = act_bank()
                    for k in range(KD):
                        last = mm(bank[:, 0:NT], w[:, k, P * (i % 2):P * (i % 2) + P], xn[:, k, :], k, KD)
                    last.then_inc(act_ready, 1)
                    outputs(i)
                pe.wait_ge(state_ready, L * ST + ST)
                bank = act_bank()
                for r in range(2):
                    pe.transpose(bank[:, P * r:P * r + P], hs[:, r, :], ident)
                for r in range(2):
                    last = pe.transpose(bank[0:ST, 256 + P * r:256 + P * r + P], hfin[:, r, :], ident)
                last.then_inc(act_ready, 1)

                pe.wait_ge(o_taken, L * 5 + 6)
                for i in range(2):
                    columns(512, 4, aT, 4, dve_bank, dve_ready)
                pe.wait_ge(y_gelu, L * 4 + 4)
                for i in range(4):
                    w = next_chunk()[:, 0:4 * 512].rearrange("p (k n) -> p k n", k=4)
                    for j in range(2):
                        for half, claim, ready in ((1, act_bank, act_ready), (0, dve_bank, dve_ready)):
                            bank = claim()
                            for k in range(4):
                                c = 256 * half + P * j
                                last = mm(bank[:, 0:NT], w[:, k, c:c + P], yT[:, k, :], k, 4)
                            last.then_inc(ready, 1)
                pe.wait_ge(merged, L * KD + KD)
                for i in range(4):
                    columns(256, 2, sg[:, 0], KD, dve_bank, dve_ready)

                small()
                pe.wait_ge(conv_in, L * 48 + 48)
                bank = act_bank(few_rows=True)
                for f in range(KF):
                    last = pe.transpose(bank[:, 20 * f:20 * f + 20], conv_rows[:, P * f:P * f + P], ident[0:20, 0:20])
                last.then_inc(act_ready, 1)
                sum_squares(1)
                pe.wait_ge(normed, L * 3 * KD + 2 * KD)
                for f in range(KF):
                    w = next_chunk()[:, 0:KD * 256].rearrange("p (k n) -> p k n", k=KD)
                    for half, claim, ready in ((0, act_bank, act_ready), (1, dve_bank, dve_ready)):
                        bank = claim()
                        for k in range(KD):
                            last = mm(bank[:, 0:NT], w[:, k, P * half:P * half + P], xn[:, k, :], k, KD)
                        last.then_inc(ready, 1)
                pe.wait_ge(act_freed, act_jobs(L, "up", KF))
                for j in range(6):
                    bank = act_bank()
                    for f in range(4 * j, min(4 * j + 4, KF)):
                        last = pe.transpose(bank[0:10, P * (f - 4 * j):P * (f - 4 * j) + P], gcol[:, f, :], ident)
                    last.then_inc(act_ready, 1)
                for o in range(KD):
                    bank = dve_bank()
                    for half in range(2):
                        w = next_chunk()[:, 0:11 * P].rearrange("p (k n) -> p k n", k=11)
                        for k in range(11):
                            kk = 11 * half + k
                            pe.wait_ge(dve_freed, dve_jobs(L, "up", kk + 1)) if o == 0 else None
                            last = mm(bank[:, 0:NT], w[:, k, :], act[:, kk, :], kk, KF)
                    last.then_inc(dve_ready, 1)

                pe.wait_ge(ple_in, L * 32 + 32)
                for k in range(2):
                    small()
                    bank = act_bank(few_rows=True)
                    for t in range(2):
                        pe.transpose(bank[:, P * t:P * t + P], p_rows[:, t, P * k:P * k + P], ident)
                    pe.transpose(bank[:, SEQ:NT], p_rows[0:NB, 2, P * k:P * k + P], ident[0:NB, 0:NB]).then_inc(act_ready, 1)
                pe.wait_ge(act_freed, act_jobs(L, "ple_in", 2))
                columns(D, KD, pT, 2, act_bank, act_ready)
                sum_squares(2)
                pe.wait_ge(normed, L * 3 * KD + 3 * KD)
                for i in range(4):
                    columns(256, 2, xn, KD, act_bank, act_ready)

            def epilogue(L, act_bank, dve_bank, next_chunk, mm):
                pe.wait_ge(h_done, DEPTH * KD + 1)
                for t in range(3):
                    m = P if t < 2 else NB
                    for j in range(2):
                        bank = act_bank() if j == 0 else dve_bank()
                        for k in range(4):
                            last = pe.transpose(bank[0:m, P * k:P * k + P], hT[:, 4 * j + k, P * t:P * t + m], ident)
                        last.then_inc(act_ready if j == 0 else dve_ready, 1)

            pe.sem_inc(weights_used, SLOTS)
            assert run(0, prologue, None, None)[0:2] == (ACT_PRO, DVE_PRO)
            with pe.Fori(0, DEPTH) as L:
                counts = run(L, layer, L * ACT_LAYER + ACT_PRO, L * DVE_LAYER + DVE_PRO)
            assert counts == (ACT_LAYER, DVE_LAYER, NCH), counts
            run(DEPTH, epilogue, DEPTH * ACT_LAYER + ACT_PRO, DEPTH * DVE_LAYER + DVE_PRO)

        @block.scalar
        def _(act_):
            n = [0]

            def fn(out, in_, func=ACT.Copy, **kw):
                return act_.activation(out, in_, func, **kw)

            def take(base):
                act_.wait_ge(act_ready, base + (n[0] + 1))
                n[0] += 1
                return bankA[(n[0] - 1) % BANKS]

            act_.sem_inc(o_taken, 1)
            for k in range(0, KD, 2):
                fn(hT[:, k, :], take(0)[:, 0:NT]).then_inc(act_freed, 1)

            def squares(L, i, done, at):
                for k in range(KD):
                    if k == 0 or i > 0:
                        act_.wait_ge(done, at(k))
                    fn(xn[:, k, :], hT[:, k, :], ACT.Square).then_inc(squared, 1)

            def std(L, i):
                act_.wait_ge(var_ready, L * 3 + i + 1)
                fn(rstd[:], rstd[:], ACT.Sqrt).then_inc(std_ready, 1)

            act_.wait_ge(consts_in, 16 * CONSTS)
            act_.wait_ge(zeroed, 2)
            with act_.Fori(0, DEPTH) as L:
                n[0] = 0
                base = L * ACT_LAYER + ACT_PRO
                squares(L, 0, h_done, lambda k: L * KD + 1)
                for s in range(NB):
                    bank = take(base)
                    fn(keys[:, s, 0:2 * PAST], bank[:]).then_inc(act_freed, 1)
                    bank = take(base)
                    fn(XT[:, :, 0:2 * NSEQ, :].rearrange("p v (g s) t -> p v g s t", g=KV)[:, :, :, s, :],
                       bank[:].rearrange("p (v g t) -> p v g t", v=2, g=KV)).then_inc(act_freed, 1)
                bank = take(base)
                for v in range(2):
                    last = fn(XT[:, v, 2 * NSEQ, :].rearrange("p (r j) -> p r j", j=16),
                              bank[:, 16 * v:16 * v + 16].unsqueeze(1).broadcast_to([P, 8, 16]))
                last.then_inc(act_freed, 1)
                act_.wait_ge(dve_freed, dve_jobs(L, "params", 1))
                fn(sm[:, 0, :], prm[:, 28 + 2 * ST:28 + 3 * ST], ACT.Exp).then_inc(dt_ready, 1)
                act_.wait_ge(trig_arg, L + 1)
                fn(sm[:, 3, :], sm[:, 2, :], ACT.Exp)
                fn(cs[:, 0], ang[:, 2], ACT.Sin, scale=-1.0, bias=c_bias[:, 1:2])
                fn(cs[:, 1], ang[:, 0], ACT.Sin).then_inc(trig_ready, 1)
                std(L, 0)
                for c0, w in QW_CHUNKS:
                    for t in range(3):
                        m = P if t < 2 else NB
                        dst, src = z[0:m, t, c0:c0 + w], take(base)[0:m, 0:w]
                        if c0 < QW:
                            dst = z[0:m, t, 0:QW].rearrange("p (c g d) -> p c g d", c=4, g=KV)[:, :, c0 // 256, :]
                            src = src.rearrange("p (c d) -> p c d", c=4)
                        fn(dst, src).then_inc(act_freed, 1)
                for i in range(4):
                    fn(uT[:, i, :], take(base)[:, 0:NT]).then_inc(act_freed, 1)
                act_.wait_ge(act_freed, act_jobs(L, "u"))
                fn(bg[:, 0:2, :], z[:, 0:2, 1280:QKV], ACT.Tanh, scale=0.5)
                fn(bg[0:NB, 2, :], z[0:NB, 2, 1280:QKV], ACT.Tanh, scale=0.5).then_inc(gates_tanh, 1)
                act_.wait_ge(hvar_ready, L + 1)
                fn(ss[:, 0:2, :], ss[:, 0:2, :], ACT.Sqrt)
                fn(ss[0:NB, 2, :], ss[0:NB, 2, :], ACT.Sqrt).then_inc(hstd_ready, 1)
                for t in range(2):
                    fn(qT[:, :, P * t:P * t + P], take(base)[:].rearrange("p (c q) -> p c q", c=4)).then_inc(act_freed, 1)
                    fn(kT[:, :, P * t:P * t + P], take(base)[:, 0:2 * P].rearrange("p (b q) -> p b q", b=2)).then_inc(act_freed, 1)
                bank = take(base)
                for g in range(KV):
                    own = qpad[64 * g:64 * g + 64, :].rearrange("p (s x) -> p s x", s=NB)
                    fn(own[:, :, 4 * g:4 * g + 4], bank[64 * g:64 * g + 64, 0:4 * NB].rearrange("p (c s) -> p s c", c=4))
                fn(keys[:, :, NEW0:NEW0 + 2], bank[:, 4 * NB:6 * NB].rearrange("p (b s) -> p s b", b=2)).then_inc(act_freed, 1)
                fn(XT[:, :, 0:2 * NSEQ, :].rearrange("p v (g s) t -> p v g s t", g=KV)[:, :, :, NB, :],
                   take(base)[:].rearrange("p (v g t) -> p v g t", v=2, g=KV)).then_inc(act_freed, 1)
                for v in range(2):
                    bank = take(base)
                    fn(pe_col[:, v:v + 1], bank[:, 2 * NSEQ * NCMP:2 * NSEQ * NCMP + 1]).then_inc(pe_bias, 1)
                    act_.wait_ge(pe_bias, L * 2 + v + 1)
                    fn(hg[:, v, :], bank[:, 0:2 * NSEQ * NCMP], ACT.Gelu_apprx_tanh, bias=pe_col[:, v:v + 1]).then_inc(act_freed, 1)
                for j in range(3):
                    fn(vcmp[:, 3 * j:3 * j + 3, :], take(base)[0:NCMP, 0:3 * KVW].rearrange("p (s d) -> p s d", s=3)).then_inc(act_freed, 1)
                act_.wait_ge(s_max, L + 1)
                for b in range(2):
                    fn(SS[:, PAST * b:PAST * b + PAST], SS[:, PAST * b:PAST * b + PAST], ACT.Exp, bias=sq4[:, 4 + b:5 + b],
                       accum_out=sq4[:, 8 + b:9 + b])
                    fn(SS[:, NEW0 + b:NEW0 + b + 1], SS[:, NEW0 + b:NEW0 + b + 1], ACT.Exp, bias=sq4[:, 4 + b:5 + b])
                fn(SS[:, CMP0:KEYS], SS[:, CMP0:KEYS], ACT.Exp, bias=sq4[:, 6:7], accum_out=sq4[:, 10:11]).then_inc(s_exp, 1)
                act_.wait_ge(c_arg, L + 1)
                fn(SP_, SP_, ACT.Exp).then_inc(c_exp, 1)

                def exps(u):
                    act_.wait_ge(p_max, L * 2 * H + u + 1)
                    nk = P * (u % 2 + 1)
                    for b in range(2):
                        last = fn(S[:, u % 2, b, 0:nk], S[:, u % 2, b, 0:nk], ACT.Exp, bias=mx[:, u % 2, b:b + 1],
                                  accum_out=sums[:, u % 2, b:b + 1])
                    last.then_inc(p_exp, 1)

                exps(0)
                bank = take(base)
                fn(PTs[:, 0:256], bank[:, 0:256])
                fn(PTs[0:NCMP, 256:320], bank[0:NCMP, 256:320])
                fn(PTs[0:NB, 320:448], bank[0:NB, 320:448]).then_inc(act_freed, 1)
                exps(1)
                act_.wait_ge(o_ready, L * 5 + 1)
                for g in range(KV):
                    last = fn(aT[64 * g:64 * g + 64, :, SEQ:NT],
                              bankO[64 * g:64 * g + 64, 0:64].rearrange("p (s h) -> p h s", s=NB)[:, 4 * g:4 * g + 4, :])
                last.then_inc(o_taken, 1)
                for u in range(2 * H):
                    if u + 1 < 2 * H and u >= 1:
                        exps(u + 1)
                    if u % 4 == 0:
                        fn(pcT[:, (u // 4) % 2, :], take(base)[0:NCMP, :]).then_inc(act_freed, 1)
                    t = u % 2
                    fn(PT[:, (u // 2) % 2, :, 0:t + 1, P * t:P * t + P],
                       take(base)[:, 0:2 * P * (t + 1)].rearrange("p (b k q) -> p b k q", b=2, k=t + 1)).then_inc(act_freed, 1)
                    if u % 4 == 0 and u >= 4:
                        c = u // 4 - 1
                        act_.wait_ge(o_ready, L * 5 + c + 2)
                        fn(aT[:, c, 0:SEQ], bankO[:, 0:SEQ]).then_inc(o_taken, 1)
                act_.wait_ge(o_ready, L * 5 + 5)
                fn(aT[:, 3, 0:SEQ], bankO[:, 0:SEQ]).then_inc(o_taken, 1)

                for i in range(ST):
                    fn(sg[:, i // KD, i % KD, :], take(base)[:, 0:NT], ACT.Tanh, scale=0.5).then_inc(act_freed, 1)
                bank = take(base)
                fn(st_out[:], bank[:, 0:2 * P].rearrange("p (r n) -> p r n", r=2))
                fn(fin_out[:], bank[0:ST, 2 * P:4 * P].rearrange("p (r n) -> p r n", r=2)).then_inc(act_freed, 1)
                for k in range(4):
                    act_.wait_ge(y_taken, L * 4 + k + 2)
                    fn(yT[:, k, :], yT[:, k, :], ACT.Gelu_apprx_tanh).then_inc(y_gelu, 1)
                for o in range(KD):
                    if o >= 2:
                        act_.wait_ge(merged, L * KD + o - 1)
                    fn(tg[:, o % 2, :], take(base)[:, 0:NT], ACT.Tanh, scale=0.5).then_inc(act_freed, 1)
                squares(L, 1, dve_freed, lambda k: dve_jobs(L, "w_o", k + 1))

                fn(cvT.rearrange("p f r -> p (f r)"), take(base)[:, 0:20 * KF]).then_inc(act_freed, 1)
                std(L, 1)

                def gelu(f):
                    act_.wait_ge(conved, L * KF + f + 1)
                    if f >= 2:
                        act_.wait_ge(dve_freed, dve_jobs(L, "up", f - 1))
                    fn(tg[:, f % 2, :], cv[:, f % 2, :], ACT.Gelu_apprx_tanh).then_inc(ff_gelu, 1)

                for f in range(KF):
                    bank = take(base)
                    if f >= 2:
                        act_.wait_ge(conved, L * KF + f - 1)
                    fn(GX[:, f % 2, 2:2 + NT], bank[:, 0:NT]).then_inc(gate_copied, 1)
                    fn(gcol[:, f, :], bank[:, SEQ - 2:NT]).then_inc(act_freed, 1)
                    if f >= 1:
                        gelu(f - 1)
                gelu(KF - 1)
                for j in range(6):
                    w = P * min(4, KF - 4 * j)
                    fn(gp_rows[:, 4 * P * j:4 * P * j + w], take(base)[0:10, 0:w]).then_inc(act_freed, 1)
                for k in range(2):
                    fn(pT[:, k, :], take(base)[:, 0:NT]).then_inc(act_freed, 1)
                squares(L, 2, dve_freed, lambda k: dve_jobs(L, "down", k + 1))
                for o in range(KD):
                    fn(plT[:, o, :], take(base)[:, 0:NT]).then_inc(act_freed, 1)
                std(L, 2)
                for o in range(KD):
                    if o >= 2:
                        act_.wait_ge(h_done, L * KD + o)
                    fn(tg[:, o % 2, :], take(base)[:, 0:NT], ACT.Tanh, scale=0.5).then_inc(act_freed, 1)
                assert n[0] == ACT_LAYER, n
            n[0] = 0
            for t in range(3):
                m = P if t < 2 else NB
                last = fn(xrows[0:m, t, 0:512], take(DEPTH * ACT_LAYER + ACT_PRO)[0:m, :]).then_inc(act_freed, 1)

        @block.vector
        def _(dve):
            n, step = [0], [0]

            def take(base):
                dve.wait_ge(dve_ready, base + (n[0] + 1))
                n[0] += 1
                return bankV[(n[0] - 1) % BANKS]

            def link(ins):
                step[0] += 1
                ins.then_inc(dve_step, 1)
                dve.wait_ge(dve_step, step[0])

            tt, ts, stt = dve.tensor_tensor, dve.tensor_scalar, dve.scalar_tensor_tensor
            MUL, ADD, SUB, MAX, MIN = ALU.mult, ALU.add, ALU.subtract, ALU.max, ALU.min

            dve.sem_inc(y_taken, 1)
            for k in range(1, KD, 2):
                ins = dve.tensor_copy(hT[:, k, :], take(0)[:, 0:NT])
                ins.then_inc(dve_freed, 1)
            dve.wait_ge(act_freed, ACT_PRO)
            dve.wait_ge(dve_freed, DVE_PRO)
            dve.sem_inc(h_done, 1)
            with dve.Fori(0, DEPTH) as L:
                n[0], step[0] = 0, 0
                dve.sem_clear(dve_step)
                base = L * DVE_LAYER + DVE_PRO

                def norm(i):
                    ts(rstd[:], take(base)[:, 0:NT], 1.0 / D, EPS, MUL, ADD).then_inc(var_ready, 1)
                    dve.wait_ge(dve_ready, base + n[0])
                    dve.wait_ge(std_ready, L * 3 + i + 1)
                    dve.reciprocal(rstd[:], rstd[:]).then_inc(dve_freed, 1)
                    dve.wait_ge(dve_freed, base + n[0])
                    for k in range(KD):
                        stt(xn[:, k, :], hT[:, k, :], prm[:, KD * i + k:KD * i + k + 1], rstd[:], MUL, MUL).then_inc(normed, 1)

                dve.wait_ge(params_in, L * 240 + 240)
                dve.tensor_copy(ssm_rows[:, 2, :].rearrange("p (g n) -> p g n", g=2),
                                dt_rows[:].unsqueeze(2).broadcast_to([ST, 2, NS_])).then_inc(dt_rows_ready, 1)
                dve.tensor_copy(prm[:], take(base)[:, 0:28 + 3 * ST]).then_inc(dve_freed, 1)
                dve.tensor_copy(h0[:].rearrange("p r x -> p (r x)"), take(base)[:, 0:2 * P]).then_inc(dve_freed, 1)
                dve.wait_ge(dve_freed, dve_jobs(L, "h0", 1))
                ar, ai = prm[:, 28:28 + ST], prm[:, 28 + ST:28 + 2 * ST]
                dt, th, ma, mag, abr, abi, den, am1, zr, zi, t1, t2 = (sm[:, j, :] for j in range(12))
                dve.wait_ge(dt_ready, L + 1)
                tt(th, dt, ai, MUL)
                link(tt(ma, dt, ar, MUL))
                link(tt(ang[:, 0], th.unsqueeze(1).broadcast_to([P, 8, ST]), c_pow[:].unsqueeze(2).broadcast_to([P, 8, ST]), MUL))
                link(ts(ang[:, 1], ang[:, 0], INV2PI, ROUND, MUL, ADD))
                link(ts(ang[:, 1], ang[:, 1], -ROUND, None, ADD))
                for part in (PI2_A, PI2_B, PI2_C):
                    link(stt(ang[:, 0], ang[:, 1], -part, ang[:, 0], MUL, ADD))
                link(ts(ang[:, 0], ang[:, 0], 3.1415925, -3.1415925, MIN, MAX))
                stt(ang[:, 2], ang[:, 0], -1.0, ang[:, 0], MUL, MAX).then_inc(trig_arg, 1)

                norm(0)

                dve.wait_ge(trig_ready, L + 1)
                tt(abr, mag, cs[:, 0, 0, :], MUL)
                tt(abi, mag, cs[:, 1, 0, :], MUL)
                tt(den, ar, ar, MUL)
                link(tt(t1, ai, ai, MUL))
                tt(den, den, t1, ADD)
                link(ts(am1, abr, -1.0, None, ADD))
                dve.reciprocal(den, den)
                tt(zr, am1, ar, MUL)
                tt(zi, abi, ar, MUL)
                tt(t1, abi, ai, MUL)
                link(tt(t2, am1, ai, MUL))
                tt(zr, zr, t1, ADD)
                link(tt(zi, zi, t2, SUB))
                tt(zr, zr, den, MUL)
                link(tt(zi, zi, den, MUL))
                dve.wait_ge(smat_in, L * 64 + 64)
                for r in range(2):
                    last = tt(cpad[:, r], cst_c[:, r].unsqueeze(2).broadcast_to([P, 4, 2, NS_]),
                              c_rmask[:].unsqueeze(1).unsqueeze(3).broadcast_to([P, 4, 2, NS_]), MUL)
                last.then_inc(c_ready, 1)
                zrb, zib = (x.unsqueeze(2).broadcast_to([P, ST, GC]) for x in (zr, zi))
                tt(bw[:, 0], bst[:, 0], zrb, MUL)
                tt(bw[:, 1], bst[:, 1], zib, MUL)
                tt(bw[:, 2], bst[:, 1], zrb, MUL)
                link(tt(bw[:, 3], bst[:, 0], zib, MUL))
                tt(bw[:, 0], bw[:, 0], bw[:, 1], SUB)
                link(tt(bw[:, 2], bw[:, 2], bw[:, 3], ADD))
                for r in range(2):
                    last = tt(bpad[:, r], bw[:, 2 * r].unsqueeze(2).broadcast_to([P, ST, 2, GC]),
                              c_gmask[:].unsqueeze(1).unsqueeze(3).broadcast_to([P, ST, 2, GC]), MUL)
                last.then_inc(b_ready, 1)
                for r in range(2):
                    ts(CT[:, r].rearrange("p k c -> p (k c)"), take(base)[:], 1.0 - 2.0 * r, None, MUL).then_inc(dve_freed, 1)
                for r in range(2):
                    dve.tensor_copy(BT[:, r].rearrange("p k c -> p (k c)"), take(base)[:]).then_inc(dve_freed, 1)

                dve.wait_ge(act_freed, act_jobs(L, "u"))

                def parts(t):
                    m = P if t < 2 else NB
                    return m, z[0:m, t, 0:QW].rearrange("p (h d) -> p h d", h=H), \
                        z[0:m, t, QW:1280].rearrange("p (j v g d) -> p j v g d", j=3, v=2, g=KV)[:, :, 0]

                for t in range(3):
                    m, zq, zk = parts(t)
                    w = PTf[0:m, 1024 * (t % 2):1024 * (t % 2) + 896]
                    tt(w[:, 0:QW].rearrange("p (h d) -> p h d", h=H), zq, zq, MUL)
                    link(tt(w[:, QW:896].rearrange("p (j g d) -> p j g d", j=3, g=KV), zk, zk, MUL))
                    link(dve.tensor_reduce(ss[0:m, t, :], w.rearrange("p (h d) -> p h d", d=HD), AX, ADD))
                ts(ss[:, 0:2, :], ss[:, 0:2, :], 1.0 / HD, EPS, MUL, ADD)
                ts(ss[0:NB, 2, :], ss[0:NB, 2, :], 1.0 / HD, EPS, MUL, ADD).then_inc(hvar_ready, 1)
                dve.wait_ge(gates_tanh, L + 1)
                ts(bg[:, 0:2, :], bg[:, 0:2, :], 0.5, 0.5, MUL, ADD)
                ts(bg[0:NB, 2, :], bg[0:NB, 2, :], 0.5, 0.5, MUL, ADD).then_inc(gates_ready, 1)
                dve.wait_ge(hstd_ready, L + 1)
                dve.reciprocal(ss[:, 0:2, :], ss[:, 0:2, :])
                link(dve.reciprocal(ss[0:NB, 2, :], ss[0:NB, 2, :]))
                for t in range(3):
                    m, zq, zk = parts(t)
                    tt(zq, zq, ss[0:m, t, 0:H].unsqueeze(2).broadcast_to([m, H, HD]), MUL)
                    link(tt(zk, zk, ss[0:m, t, H:14].rearrange("p (j g) -> p j g", j=3).unsqueeze(3).broadcast_to([m, 3, KV, HD]), MUL))
                    tt(zq, zq, gains[0:m, 0:1, :].broadcast_to([m, H, HD]), MUL)
                    link(tt(zk, zk, gains[0:m, 1:4, :].unsqueeze(2).broadcast_to([m, 3, KV, HD]), MUL))
                    qc, qs = (PTf[0:m, 512 * j:512 * j + 512].rearrange("p (h d) -> p h d", h=H) for j in range(2))
                    kc, ksn = (PTf[0:m, 1024 + 256 * j:1280 + 256 * j].rearrange("p (j g d) -> p j g d", j=2, g=KV) for j in range(2))
                    zk = zk[:, 1:3]
                    co, si = c_cos[0:m, t, :], c_sin[0:m, t, :]
                    hf = HD // 2
                    tt(qc, zq, co.unsqueeze(1).broadcast_to([m, H, HD]), MUL)
                    for a, b in ((0, hf), (hf, 0)):
                        tt(qs[:, :, a:a + hf], zq[:, :, b:b + hf], si[:, a:a + hf].unsqueeze(1).broadcast_to([m, H, hf]), MUL)
                    tt(kc, zk, co.unsqueeze(1).unsqueeze(1).broadcast_to([m, 2, KV, HD]), MUL)
                    for a, b in ((0, hf), (hf, 0)):
                        last = tt(ksn[:, :, :, a:a + hf], zk[:, :, :, b:b + hf],
                                  si[:, a:a + hf].unsqueeze(1).unsqueeze(1).broadcast_to([m, 2, KV, hf]), MUL)
                    link(last)
                    tt(zq, qc, qs, ADD)
                    tt(zk, kc, ksn, ADD).then_inc(roped, 1)

                dve.wait_ge(act_freed, act_jobs(L, "turn_qk"))
                tt(upad[:], uT[:, :, SEQ:NT].unsqueeze(2).broadcast_to([P, 4, 4, NB]),
                   c_qmask[:].unsqueeze(1).unsqueeze(3).broadcast_to([P, 4, 4, NB]), MUL).then_inc(u_spread, 1)

                bank = take(base)
                tt(g64[:], bank[0:64, 0:24].rearrange("p (h b) -> p h b", h=H), c_head[:].unsqueeze(2).broadcast_to([64, H, 3]), MUL).then_inc(dve_freed, 1)
                dve.wait_ge(dve_freed, base + n[0])
                link(dve.tensor_reduce(gg[:], g64[:].rearrange("p h b -> p b h"), AX, ADD))

                bank = take(base)
                for r, table in ((0, c_ccos), (1, c_csin)):
                    last = tt(kct[:, r].rearrange("p (s n) -> p s n", s=NSEQ), bank[:, 256 * r:256 * r + NSEQ * NCMP].rearrange("p (s n) -> p s n", s=NSEQ),
                              table[:].unsqueeze(1).broadcast_to([P, NSEQ, NCMP]), MUL)
                last.then_inc(dve_freed, 1)
                dve.wait_ge(dve_freed, base + n[0])
                kv_ = kct.rearrange("p r (s n) -> p r s n", s=NSEQ)
                tt(keys[:, :, CMP0:KEYS], kv_[:, 0, 0:NB], kv_[:, 1, 0:NB], ADD)
                tt(kcmp[:], kv_[:, 0, NB], kv_[:, 1, NB], ADD).then_inc(kcmp_ready, 1)

                ts(SS[:, 0:NEW0], take(base)[0:64, :], SCALE, None, MUL).then_inc(dve_freed, 1)
                ts(SS[:, NEW0:KEYS], take(base)[0:64, 0:KEYS - NEW0], SCALE, None, MUL).then_inc(dve_freed, 1)
                dve.wait_ge(dve_freed, base + n[0])
                dve.tensor_reduce(sq4[:, 0:2], SS[:, 0:NEW0].rearrange("p (b k) -> p b k", b=2), AX, MAX)
                link(dve.tensor_reduce(sq4[:, 2:3], SS[:, CMP0:KEYS], AX, MAX))
                link(tt(sq4[:, 0:2], sq4[:, 0:2], SS[:, NEW0:CMP0], MAX))
                ts(sq4[:, 4:7], sq4[:, 0:3], -1.0, None, MUL).then_inc(s_max, 1)
                sc = SP_.rearrange("p (t h) n -> p t h n", t=2)
                for g in range(KV):
                    bt = take(base)[:, 0:8 * NCMP].rearrange("p (t c n) -> p t c n", t=2, c=4)
                    for t in range(2):
                        last = stt(sc[:, t, 4 * g:4 * g + 4], bt[:, t], SCALE,
                                   c_cmask[:, 0, t, :].unsqueeze(1).broadcast_to([P, 4, NCMP]), MUL, ADD)
                    last.then_inc(dve_freed, 1)
                dve.wait_ge(dve_freed, base + n[0])
                link(dve.tensor_reduce(cmx[:], SP_, AX, MAX))
                tt(SP_, SP_, cmx[:].unsqueeze(2).broadcast_to([P, 16, NCMP]), SUB).then_inc(c_arg, 1)

                def scores(u):
                    t = u % 2
                    nk = P * (t + 1)
                    bank = take(base)
                    if u >= 2:
                        dve.wait_ge(act_freed, probs_turned(L, u - 2))
                    stt(S[:, t, :, 0:nk], bank[:, 0:2 * nk].rearrange("p (b k) -> p b k", b=2), SCALE,
                        c_mask[:, SEQ - nk:SEQ].unsqueeze(1).broadcast_to([P, 2, nk]), MUL, ADD).then_inc(dve_freed, 1)
                    dve.wait_ge(dve_freed, base + n[0])
                    dve.tensor_reduce(mx[:, t, 0:2], S[:, t, :, 0:nk], AX, MAX, negate=True).then_inc(p_max, 1)

                def weigh(u):
                    idx, t = divmod(u, 2)
                    c, g = divmod(idx, 2)
                    h = 4 * g + c
                    nk = P * (t + 1)
                    dve.wait_ge(p_exp, L * 2 * H + u + 1)
                    link(dve.reciprocal(sums[:, t, 2:4], sums[:, t, 0:2]))
                    link(tt(sums[:, t, 2:4], sums[:, t, 2:4], bg[:, t, 3 * h + 1:3 * h + 3], MUL))
                    tt(S[:, t, :, 0:nk], S[:, t, :, 0:nk], sums[:, t, 2:4].unsqueeze(2).broadcast_to([P, 2, nk]), MUL).then_inc(p_prob, 1)

                scores(0)
                dve.wait_ge(s_exp, L + 1)
                link(tt(sq4[:, 8:10], sq4[:, 8:10], SS[:, NEW0:CMP0], ADD))
                link(ts(sq4[:, 8:11], sq4[:, 8:11], 1e-30, None, MAX))
                link(dve.reciprocal(sq4[:, 12:15], sq4[:, 8:11]))
                tt(sq4[:, 12:14], sq4[:, 12:14], gg[:, 1:3], MUL)
                link(tt(sq4[:, 14:15], sq4[:, 14:15], gg[:, 0:1], MUL))
                link(tt(SS[:, NEW0:CMP0], SS[:, NEW0:CMP0], sq4[:, 12:14], MUL))
                sv = SS[:, 0:NEW0].rearrange("p (b k) -> p b k", b=2)
                tt(sv, sv, sq4[:, 12:14].unsqueeze(2).broadcast_to([64, 2, PAST]), MUL)
                ts(SS[:, CMP0:KEYS], SS[:, CMP0:KEYS], sq4[:, 14:15], None, MUL)
                for b in range(2):
                    last = ts(snew[:, b, :], c_diag[:], SS[:, NEW0 + b:NEW0 + b + 1], None, MUL)
                last.then_inc(s_prob, 1)
                scores(1)
                dve.wait_ge(c_exp, L + 1)
                for t in range(2):
                    last = tt(sc[:, t], sc[:, t], c_cmask[:, 1, t, :].unsqueeze(1).broadcast_to([P, H, NCMP]), MUL)
                link(last)
                link(dve.tensor_reduce(csum[:], SP_, AX, ADD))
                link(ts(csum[:], csum[:], 1e-30, None, MAX))
                link(dve.reciprocal(csum[:], csum[:]))
                link(tt(csum[:].rearrange("p (t h) -> p t h", t=2), csum[:].rearrange("p (t h) -> p t h", t=2),
                        bg[:, 0:2, 0:22:3], MUL))
                tt(SP_, SP_, csum[:].unsqueeze(2).broadcast_to([P, 16, NCMP]), MUL).then_inc(c_prob, 1)
                weigh(0)
                for u in range(1, 2 * H):
                    if u + 1 < 2 * H:
                        scores(u + 1)
                    weigh(u)

                bank = take(base)
                def over(x):
                    return x.unsqueeze(1).broadcast_to([P, NB, ST])
                def rows(x):
                    return x.rearrange("p (s i) -> p s i", s=NB)
                for r in range(2):
                    w = W1[:, r, 0:P], W2[:, r, 0:P]
                    tt(rows(w[0]), rows(h0[:, r]), over(abr), MUL)
                    link(tt(rows(w[1]), rows(h0[:, 1 - r]), over(abi), MUL))
                    link(tt(w[0], w[0], w[1], ADD if r else SUB))
                    last = tt(hs[:, r, :].rearrange("p (s i) -> p i s", s=NB), w[0].rearrange("p (s i) -> p i s", s=NB),
                              bank[:, P * r:P * r + P].rearrange("p (i s) -> p i s", s=NB), ADD)
                last.then_inc(dve_freed, 1)
                dve.wait_ge(dve_freed, base + n[0])

                for i in range(ST):
                    q = i // 2
                    bank = take(base)
                    if i % 2 == 0:
                        dve.wait_ge(rot_ready, L * (ST // 2) + q + 1)
                    bu = bank[:].rearrange("p (c t) -> p c t", c=2)
                    co, si = (rot[:, q % 2, j, i % 2, :].unsqueeze(1).broadcast_to([P, 2, SEQ]) for j in range(2))
                    tt(W1, bu, co, MUL)
                    tt(W2, bu, si, MUL).then_inc(dve_freed, 1)
                    dve.wait_ge(dve_freed, base + n[0])
                    tt(W1[:, 0], W1[:, 0], W2[:, 1], ADD)
                    link(tt(W1[:, 1], W1[:, 1], W2[:, 0], SUB))
                    for c in range(2):
                        last = dve.tensor_tensor_scan(G[:, c], mag[:, i:i + 1].broadcast_to([P, SEQ]), W1[:, c], 0.0, MUL, ADD)
                    link(last)
                    tt(W1, G, co, MUL)
                    last = tt(W2, G, si, MUL)
                    if i % 2:
                        last.then_inc(rot_used, 1)
                        dve.wait_ge(rot_used, L * (ST // 2) + q + 1)
                    else:
                        link(last)
                    if i >= 2:
                        dve.wait_ge(y_ready, L * ST + i - 1)
                    tt(HH[:, i % 2, 0], W1[:, 0], W2[:, 1], SUB)
                    link(tt(HH[:, i % 2, 1], W1[:, 1], W2[:, 0], ADD))
                    dve.tensor_copy(hfin[:, :, i:i + 1], HH[:, i % 2, :, SEQ - 1:SEQ]).then_inc(state_ready, 1)
                    if i % 4 == 3:
                        k = i // 4
                        dve.wait_ge(y_ready, L * ST + i + 1)
                        stt(yT[:, k, :], uT[:, k, :], prm[:, 24 + k:25 + k], bankY[:, 0:NT], MUL, ADD).then_inc(y_taken, 1)

                for o in range(KD):
                    stt(sg[:, 0, o, :], sg[:, 0, o, :], 1.0, take(base)[:, 0:NT], ADD, MUL).then_inc(dve_freed, 1)
                dve.wait_ge(dve_freed, base + n[0])
                for o in range(KD):
                    bank = take(base)
                    dve.wait_ge(act_freed, act_jobs(L, "glu", o + 1))
                    stt(cv[:, o % 2, :], tg[:, o % 2, :], 1.0, bank[:, 0:NT], ADD, MUL).then_inc(dve_freed, 1)
                    dve.wait_ge(dve_freed, base + n[0])
                    link(stt(cv[:, o % 2, :], sg[:, 1, o, :], 1.0, cv[:, o % 2, :], ADD, MUL))
                    stt(sg[:, 0, o, :], cv[:, o % 2, :], 0.5, sg[:, 0, o, :], MUL, ADD).then_inc(merged, 1)
                for o in range(KD):
                    stt(hT[:, o, :], take(base)[:, 0:NT], 0.5, hT[:, o, :], MUL, ADD).then_inc(dve_freed, 1)

                norm(1)
                dve.wait_ge(act_freed, act_jobs(L, "conv", 1))

                def conv(f):
                    dve.wait_ge(gate_copied, L * KF + f + 1)
                    if f >= 2:
                        dve.wait_ge(ff_gelu, L * KF + f - 1)
                    x, c = GX[:, f % 2, :], cv[:, f % 2, :]
                    tap = [cvT[:, f, 16 + j:17 + j] for j in range(4)]
                    old = cvT[:, f, 0:16].rearrange("p (s j) -> p s j", j=2)
                    link(ts(c, x[:, 2:2 + NT], tap[2], tap[3], MUL, ADD))
                    stt(c[:, 0:SEQ], x[:, 1:1 + SEQ], tap[1], c[:, 0:SEQ], MUL, ADD)
                    link(stt(c[:, SEQ:NT], old[:, :, 1], tap[1], c[:, SEQ:NT], MUL, ADD))
                    stt(c[:, 0:SEQ], x[:, 0:SEQ], tap[0], c[:, 0:SEQ], MUL, ADD)
                    stt(c[:, SEQ:NT], old[:, :, 0], tap[0], c[:, SEQ:NT], MUL, ADD).then_inc(conved, 1)

                def gated(f):
                    bank = take(base)
                    dve.wait_ge(ff_gelu, L * KF + f + 1)
                    tt(act[:, f, :], tg[:, f % 2, :], bank[:, 0:NT], MUL).then_inc(dve_freed, 1)

                for f in range(KF):
                    conv(f)
                    if f >= 1:
                        gated(f - 1)
                gated(KF - 1)
                for o in range(KD):
                    tt(hT[:, o, :], take(base)[:, 0:NT], hT[:, o, :], ADD).then_inc(dve_freed, 1)

                norm(2)
                for o in range(KD):
                    dve.wait_ge(act_freed, act_jobs(L, "ple_gate", o + 1))
                    link(stt(cv[:, o % 2, :], tg[:, o % 2, :], 1.0, plT[:, o, :], ADD, MUL))
                    stt(hT[:, o, :], cv[:, o % 2, :], 0.5, hT[:, o, :], MUL, ADD).then_inc(h_done, 1)
                assert n[0] == DVE_LAYER, n
            n[0] = 0
            for t in range(3):
                m = P if t < 2 else NB
                dve.tensor_copy(xrows[0:m, t, 512:D], take(DEPTH * DVE_LAYER + DVE_PRO)[0:m, :]).then_inc(dve_freed, 1)


def constants():
    import numpy as np
    f = np.float32
    half = HD // 2
    inv = (f(10000.0) ** (-np.arange(half, dtype=f) / f(half))).astype(f)

    def rot(pos):
        ang = pos.astype(f)[:, None] * inv[None, :]
        co, si = np.cos(ang).astype(f), np.sin(ang).astype(f)
        return np.concatenate([co, co], 1), np.concatenate([-si, si], 1)

    pos = np.arange(3 * P)
    pos[2 * P:] = PAST
    co, si = rot(pos)
    cend, send = rot(np.arange(NCMP) * CS + CB - 1)
    q, k = np.arange(P)[:, None], np.arange(P)[None, :]
    mask = np.concatenate([np.zeros((P, P), f), np.where(k <= q, 0, NEG).astype(f)], 1)
    seen = np.stack([(np.arange(NCMP) * CS + CB - 1)[None, :] <= q + P * t for t in range(2)], 1)
    row = np.arange(64)
    c = {
        "ident": np.eye(P), "mask": mask,
        "cos": co.reshape(3, P, HD).transpose(1, 0, 2), "sin": si.reshape(3, P, HD).transpose(1, 0, 2),
        "ccos": np.concatenate([cend.T, cend.T]), "csin": np.concatenate([send.T, send.T]),
        "cmask": np.stack([np.where(seen, 0, NEG), seen], 1),
        "ones": np.ones((P, P)),
        "gmask": np.stack([np.arange(P) < 64, np.arange(P) >= 64], 1),
        "rmask": np.stack([np.arange(P) // 16 % 2 == 0, np.arange(P) // 16 % 2 == 1], 1),
        "qmask": np.arange(P)[:, None] // 32 == np.arange(4)[None, :],
        "pow": np.tile(2.0 ** np.arange(8), (P, 1)),
        "sel": np.arange(NB)[:, None] == row[None, :] // 8,
        "diag": row[:, None] // 8 == np.arange(NB)[None, :],
        "head": row[:, None] % 8 == np.arange(8)[None, :],
        "bias": np.tile(np.array([EPS, np.pi / 2]), (P, 1)),
    }
    return {k: np.ascontiguousarray(v.astype(f)) for k, v in c.items()}


OUT_SHAPES = [(1, SEQ, D), (NB, 1, D)] + [(DEPTH, 1, SEQ, 2, KV, HD)] * 3 + [(DEPTH, 1, NG, NS_)] * 2 + \
    [(DEPTH, 1, 2, FF)] + [(DEPTH, NB, 1, 2, KV, HD)] * 2 + [(DEPTH, NB, PAST, 2, KV, HD)] + \
    [(DEPTH, NB, NG, NS_)] * 2 + [(DEPTH, NB, 2, FF)]


def kernel(**inputs):
    import numpy as np
    import concourse.bacc as bacc
    from concourse.bass_utils import run_bass_kernel_spmd as run

    nc = bacc.Bacc("TRN2", target_bir_lowering=False, num_devices=1)
    arrays, A, C, O = {}, {}, {}, []
    for name, value in inputs.items():
        a = np.ascontiguousarray(value)
        arrays[f"in_{name}_dram"] = a
        A[name] = nc.dram_tensor(f"in_{name}_dram", a.shape, mybir.dt.from_np(a.dtype), kind="ExternalInput").ap()
    for name, a in constants().items():
        arrays[f"c_{name}_dram"] = a
        C[name] = nc.dram_tensor(f"c_{name}_dram", a.shape, F32, kind="ExternalInput").ap()
    for i, shape in enumerate(OUT_SHAPES):
        O.append(nc.dram_tensor(f"out_{i}_dram", shape, F32, kind="ExternalOutput").ap())
    trunk(nc, A, C, O)
    r = run(nc, [arrays], core_ids=[0])
    return tuple(r.results[0][f"out_{i}_dram"] for i in range(len(OUT_SHAPES)))
```

```python
from contextlib import ExitStack

import concourse.bass as bass
from concourse import mybir

F32 = mybir.dt.float32
I32 = mybir.dt.int32
ALU = mybir.AluOpType
ACT = mybir.ActivationFunctionType
AX = mybir.AxisListType.X
ds = bass.ds

P = 128
D, DEPTH, SEQ, NB = 1024, 2, 256, 8
NT = SEQ + NB
KD = D // P
H, KV, HD = 8, 2, 64
QW, KVW = H * HD, KV * HD
PAGE, PAGES = 128, 2
PAST = PAGE * PAGES
CB, CS, NCMP = 32, 16, (SEQ - 32) // 16 + 1
SSMW, GC, NG, NS_ = 512, 16, 32, 64
ST = NG * NS_ // P
FF = 2816
KF = FF // P
PLE = 256
QKV = QW + 6 * KVW + 3 * H
U0, GA0 = QKV, QKV + SSMW
EPS = 1e-6
SCALE = HD ** -0.5
NEG = -1e30
NSEQ = NB + 1
KEYS = 2 * (PAST + 1) + NCMP
NEW0, CMP0 = 2 * PAST, 2 * PAST + 2
XR = 2 * NSEQ + 1
INV2PI = 0.15915494309189535
CONSTS = 16
ROUND = 12582912.0
PI2_A, PI2_B, PI2_C = 6.28125, 0.0019350051879882812, 3.0199157663446332e-07

SLOT = 2240
SLOTS = 5
QW_CHUNKS = [(256 * i, 256) for i in range(4)] + [(1024, 280)]

GATES_AT = (5, 8, 11)

ACT_PRO, DVE_PRO = 4, 4
BANKS = 3

def offsets(stages):
    at, out = 0, {}
    for name, n in stages:
        out[name] = at
        at += n
    return out, at


A_AT, ACT_LAYER = offsets((
    ("u", 4), ("qkv", 3 * len(QW_CHUNKS) + 2 * NB + 2 * len(GATES_AT)), ("pe", 1), ("states", 1),
    ("gates_rotary", 4), ("turn_qk", 9), ("cmp", 1), ("hidden", 2),
    ("v_cmp", 3), ("gates_softmax", 2), ("s_probs", 1), ("p_probs", 2 * H + 4), ("glu", KD), ("conv", 1),
    ("up", KF), ("gate_rows", 6), ("ple_in", 2), ("ple", KD), ("ple_gate", KD)))
V_AT, DVE_LAYER = offsets((
    ("params", 1), ("norm0", 1), ("c", 2), ("b", 2), ("h0", 1), ("s_drive", 1),
    ("drive", ST), ("s_gates", 1), ("k_cmp", 1), ("s_scores", 2), ("c_scores", 2), ("p_scores", 2 * H), ("w_a", KD), ("glu", KD), ("w_o", KD),
    ("norm1", 1), ("up", KF), ("down", KD), ("norm2", 1)))


def act_jobs(L, stage, n=0):
    return L * ACT_LAYER + (ACT_PRO + A_AT[stage] + n)


def dve_jobs(L, stage, n=0):
    return L * DVE_LAYER + (DVE_PRO + V_AT[stage] + n)


def caches_turned(L, s):
    return act_jobs(L, "qkv", 4 * s + 4 + 2 * sum(j <= 2 * s for j in GATES_AT))


def probs_turned(L, u):
    return act_jobs(L, "p_probs", u + u // 4 + 2)


def weight_chunks():
    names = [("u", i) for i in range(2)]
    for i in range(5):
        names += [("qkv", i)]
        if 3 * i + 2 in GATES_AT:
            names += [("gate", GATES_AT.index(3 * i + 2))]
    before_cmp = len(GATES_AT) + 4
    names += [("gate", i) for i in range(len(GATES_AT), before_cmp)]
    names += [("cmp", i) for i in range(2)]
    names += [("gate", i) for i in range(before_cmp, 8)]
    names += [("w_a", i) for i in range(2)]
    names += [("glu", i) for i in range(4)]
    names += [("w_o", i) for i in range(4)]
    names += [("up", i) for i in range(22)]
    names += [("down", i) for i in range(16)]
    names += [("ple", 0)]
    names += [("ple_gate", i) for i in range(4)]
    return names


V_LOADS = 16 * (NB * PAGES + 2)

CHUNKS = weight_chunks()
NCH = len(CHUNKS)
assert NCH % SLOTS == 0


def trunk(nc, A, C, O):
    ctx = ExitStack()
    with ctx:
        def sb(name, shape, dt=F32):
            return ctx.enter_context(nc.sbuf_tensor(name, shape, dt))

        def sem(name):
            return ctx.enter_context(nc.semaphore(name))

        ring = sb("ring", [P, SLOTS, SLOT])
        hT = sb("hT", [P, KD, NT])
        xn = sb("xn", [P, KD, NT])
        z = sb("z", [P, 3, QKV])
        vpast = sb("vpast", [P, 2, NB, PAGES, KVW])
        prompt_cmp = sb("prompt_cmp", [P, 4 * KVW])
        R1 = sb("R1", [P, KF * NT])
        kall = sb("kall", [P, NB * KEYS])
        sg = sb("sg", [P, 2, KD, NT])
        kT = sb("kT", [P, 2, SEQ])
        qpad = sb("qpad", [P, NB * 64 + 64])
        Sf = sb("Sf", [P, 6 * SEQ])
        PT = sb("PT", [P, 2, 2, 2, SEQ])
        pcw = sb("pcw", [P, 2, 512])
        aT = sb("aT", [P, 4, NT])
        uT = sb("uT", [P, 4, NT])
        upad = sb("upad", [P, 4, 4, NB])
        BT = sb("BT", [P, 2, 4, P])
        CT = sb("CT", [P, 2, 4, P])
        prm_rows = sb("prm_rows", [28, P])
        ssm_rows = sb("ssm_rows", [ST, 3, P])
        dt_rows = sb("dt_rows", [ST, 2])
        h0_rows = sb("h0_rows", [P, 2, P])
        prm = sb("prm", [P, 28 + 3 * ST])
        gains = sb("gains", [P, 4, HD])
        w2 = sb("w2", [P, 3, HD])
        pe_rows = sb("pe_rows", [16, 2, P])
        pe_col = sb("pe_col", [P, 2])
        rstd = sb("rstd", [P, NT])
        ss = sb("ss", [P, 3, 14])
        cs = sb("cs", [P, 2, 8, ST])
        sm = sb("sm", [P, 16, ST])
        h0 = sb("h0", [P, 2, NB * ST])
        hs = sb("hs", [P, 2, NB * ST])
        hfin = sb("hfin", [P, 2, ST])
        kcmp = sb("kcmp", [P, NCMP])
        mx = sb("mx", [P, 4, 2])
        sums = sb("sums", [P, 4, 4])
        cmx = sb("cmx", [P, 16])
        csum = sb("csum", [P, 16])
        bg = sb("bg", [P, 3, 24])
        snew = sb("snew", [64, 2, NB])
        sq4 = sb("sq4", [64, 16])
        gg = sb("gg", [64, 3])
        g64 = sb("g64", [64, 8, 3])
        GX = sb("GX", [P, 2, 2 + NT])
        warm = sb("warm", [P, 1])
        pt_sb = sb("pt_sb", [1, NB * PAGES], I32)
        c_id = sb("c_id", [P, P])
        c_mask = sb("c_mask", [P, SEQ])
        c_cos = sb("c_cos", [P, 3, HD])
        c_sin = sb("c_sin", [P, 3, HD])
        c_ccos = sb("c_ccos", [P, NCMP])
        c_csin = sb("c_csin", [P, NCMP])
        c_cmask = sb("c_cmask", [P, 2, 2, NCMP])
        c_ones = sb("c_ones", [P, P])
        c_gmask = sb("c_gmask", [P, 2])
        c_rmask = sb("c_rmask", [P, 2])
        c_qmask = sb("c_qmask", [P, 4])
        c_pow = sb("c_pow", [P, 8])
        c_sel = sb("c_sel", [NB, 64])
        c_diag = sb("c_diag", [64, NB])
        c_head = sb("c_head", [64, 8])
        c_bias = sb("c_bias", [P, 2])

        xrows = R1[:, 0:3 * D].rearrange("p (t d) -> p t d", t=3)
        XT = R1[:, 0:2 * XR * P].rearrange("p (v r t) -> p v r t", v=2, r=XR)
        vpf = vpast[:].rearrange("p b s g k -> p (b s g k)")
        rot = vpf[:, 0:2048].rearrange("p (b c i t) -> p b c i t", b=2, c=2, i=2)
        rotw = vpf[:, 2048:3072].rearrange("p (w x) -> p w x", w=2)
        rot0 = vpf[:, 3072:4096].rearrange("p (c i t) -> p c i t", c=2, i=ST)
        W1 = R1[:, 2 * XR * P:2 * XR * P + 512].rearrange("p (c t) -> p c t", c=2)
        W2 = Sf[:, 2 * SEQ:4 * SEQ].rearrange("p (c t) -> p c t", c=2)
        G = kT[:]
        HH = pcw[:].rearrange("p b x -> p (b x)").rearrange("p (b c t) -> p b c t", b=2, c=2)
        act = R1[:, 0:KF * NT].rearrange("p (f t) -> p f t", f=KF)
        keys = kall[:].rearrange("p (s k) -> p s k", s=NB)
        conv_rows = kall[0:20, 0:FF]
        gp_rows = kall[0:10, 0:FF]
        sgf = sg[:].rearrange("p g k t -> p (g k t)")
        bst = sgf[:, 0:512].rearrange("p (r i c) -> p r i c", r=2, i=ST)
        bpad = sgf[:, 512:1536].rearrange("p (r i g c) -> p r i g c", r=2, i=ST, g=2)
        bw = sgf[:, 1536:2560].rearrange("p (w i c) -> p w i c", w=4, i=ST)
        cst_c = sgf[:, 2560:3072].rearrange("p (r k s) -> p r k s", r=2, k=4)
        cpad = sgf[:, 3072:4096].rearrange("p (r k g s) -> p r k g s", r=2, k=4, g=2)
        pT = z[:, 1, 0:2 * NT].rearrange("p (k t) -> p k t", k=2)
        p_rows = z[:, 2, 0:3 * PLE].rearrange("p (t k) -> p t k", t=3)
        plT = sg[:, 0]
        qT = aT[:, :, 0:SEQ]

        def S(u):
            at, nk = (0, SEQ, 3 * SEQ, 4 * SEQ)[u % 4], P * (u % 2 + 1)
            return Sf[:, at:at + 2 * nk].rearrange("p (b k) -> p b k", b=2)

        ang = Sf[:, 0:24 * ST].rearrange("p (w k i) -> p w k i", w=3, k=8)
        hg = Sf[:, 0:4 * NSEQ * NCMP].rearrange("p (v n) -> p v n", v=2)
        PTf = PT[:].rearrange("p a b c q -> p (a b c q)")
        kst = PTf[:, 0:1024].rearrange("p (b v g k) -> p b v g k", b=2, v=2, g=PAGES)
        cst = PTf[:, 1024:2048].rearrange("p (b x) -> p b x", b=2)
        SS = R1[0:64, 3072:3072 + KEYS]
        PTs = R1[:, 3632:4080]
        SP_ = R1[:, 4080:4320].rearrange("p (h n) -> p h n", h=16)
        vcmp = R1[0:NCMP, 4320:5472].rearrange("p (s k) -> p s k", s=NSEQ)
        kct = R1[:, 5472:5742].rearrange("p (r n) -> p r n", r=2)
        st_out = h0_rows
        fin_out = ssm_rows[:, 0:2, :]
        tg = PTf[:, 0:2 * NT].rearrange("p (b t) -> p b t", b=2)
        cv = PTf[:, 2 * NT:4 * NT].rearrange("p (b t) -> p b t", b=2)
        gcol = PTf[:, 4 * NT:4 * NT + 10 * KF].rearrange("p (f t) -> p f t", f=KF)
        cvT = PTf[:, 4 * NT + 10 * KF:4 * NT + 30 * KF].rearrange("p (f t) -> p f t", f=KF)
        ident = c_id[:]

        bankA = [ctx.enter_context(nc.psum_tensor(f"bank_act{i}", [P, 512], F32)) for i in range(BANKS)]
        bankV = [ctx.enter_context(nc.psum_tensor(f"bank_dve{i}", [P, 512], F32)) for i in range(BANKS)]
        bankO = ctx.enter_context(nc.psum_tensor("bank_o", [P, 512], F32))
        bankY = ctx.enter_context(nc.psum_tensor("bank_y", [P, 512], F32))

        consts_in = sem("consts_in")
        x_in, ident_in = sem("x_in"), sem("ident_in")
        weights_in = [sem(f"weights_in{i}") for i in range(SLOTS)]
        weights_used = sem("weights_used")
        act_ready, act_freed = sem("act_ready"), sem("act_freed")
        dve_ready, dve_freed = sem("dve_ready"), sem("dve_freed")
        dve_step, pool_step = sem("dve_step"), sem("pool_step")
        params_in, more_in = sem("params_in"), sem("more_in")
        smat_in = sem("smat_in")
        h0_in = sem("h0_in")
        k_in = [sem("k_in0"), sem("k_in1")]
        kw_in = [sem("kw_in0"), sem("kw_in1")]
        v_in = sem("v_in")
        cmp_in = [sem("cmp_in0"), sem("cmp_in1")]
        rows_out, cmp_out = sem("rows_out"), sem("cmp_out")
        rows_back = sem("rows_back")
        pe_in = sem("pe_in")
        conv_in = sem("conv_in")
        ple_in = sem("ple_in")
        states_out, conv_out, y_out = sem("states_out"), sem("conv_out"), sem("y_out")
        copies_out = sem("copies_out")
        squared, added = sem("squared"), sem("added")
        std_ready = sem("std_ready")
        normed = sem("normed")
        dt_rows_ready = sem("dt_rows_ready")
        dt_ready, trig_arg, trig_ready = sem("dt_ready"), sem("trig_arg"), sem("trig_ready")
        b_ready, c_ready = sem("b_ready"), sem("c_ready")
        rot_ready, rot_used = sem("rot_ready"), sem("rot_used")
        zeroed = sem("zeroed")
        gates_tanh, gates_ready = sem("gates_tanh"), sem("gates_ready")
        hvar_ready, hstd_ready = sem("hvar_ready"), sem("hstd_ready")
        roped, u_spread = sem("roped"), sem("u_spread")
        pe_bias = sem("pe_bias")
        kcmp_ready = sem("kcmp_ready")
        s_max, s_exp, s_prob = sem("s_max"), sem("s_exp"), sem("s_prob")
        c_arg, c_exp, c_prob = sem("c_arg"), sem("c_exp"), sem("c_prob")
        p_max, p_exp, p_prob = sem("p_max"), sem("p_exp"), sem("p_prob")
        o_ready, o_taken = sem("o_ready"), sem("o_taken")
        state_ready = sem("state_ready")
        y_ready, y_taken, y_gelu = sem("y_ready"), sem("y_taken"), sem("y_gelu")
        merged = sem("merged")
        h_done = sem("h_done")
        gate_copied, conved, ff_gelu = sem("gate_copied"), sem("conved"), sem("ff_gelu")

        block = ctx.enter_context(nc.Block())
        (y_prompt, y_sample, cmp_p, sel_p, win_p, re_p, im_p, conv_p,
         cmp_s, sel_s, win_s, re_s, im_s, conv_s) = O

        @block.sync
        def _(sp):
            def cols(name, k0, nk, c0, n):
                w = A[name].rearrange("l (k p) n -> p (l k) n", p=P)
                per = A[name].shape[1] // P
                return lambda L: w[:, ds(L * per + k0, nk), c0:c0 + n]

            def heads(name, c0, n, half):
                w = A[name].rearrange("l (g c d) n -> d (l g) c n", g=KV, c=4)
                return lambda L: w[:, ds(L * KV + half, 1), :, c0:c0 + n]

            with nc.allow_non_contiguous_dma(reason="short rows"):
                sp.dma_start(c_id[:], C["ident"]).then_inc(ident_in, 16)
                for t, name in ((c_ones, "ones"), (c_pow, "pow"), (c_bias, "bias"), (c_mask, "mask"), (c_cos, "cos"), (c_sin, "sin"),
                                (c_ccos, "ccos"), (c_csin, "csin"), (c_cmask, "cmask"),
                                (c_gmask, "gmask"), (c_rmask, "rmask"), (c_qmask, "qmask"), (c_sel, "sel"),
                                (c_diag, "diag"), (c_head, "head")):
                    sp.dma_start(t[:], C[name]).then_inc(consts_in, 16)
                sp.dma_start(pt_sb[:], A["page_table"].rearrange("s (a g) -> a (s g)", a=1)).then_inc(consts_in, 16)
            with sp.Fori(0, DEPTH) as L:
                for m, (name, i) in enumerate(CHUNKS):
                    slot = m % SLOTS
                    count = L * NCH + (m + 2)
                    if name in ("u", "qkv"):
                        count = sp.to_reg(count)
                        sp.wait_ge(ident_in, 16)
                    sp.wait_ge(weights_used, count)

                    def put(k, n, off, width, src, rows=slice(0, P)):
                        dst = ring[rows, slot, 0:k * width].rearrange("p (k n) -> p k n", k=k)
                        sp.dma_start(dst[:, :, off:off + n], src).then_inc(weights_in[slot], 16)

                    if name == "cmp":
                        w = A[("cmp_wk1", "cmp_wv1")[i]].rearrange("l (j a) d f -> (a d) (l j) f", a=2)
                        for j in (0, 8):
                            sp.dma_start(ring[:, slot, j * P:(j + 8) * P].rearrange("p (j n) -> p j n", j=8),
                                         w[:, ds(L * 16 + j, 8), :]).then_inc(weights_in[slot], 16)
                    elif name == "qkv":
                        c0, n = QW_CHUNKS[i]
                        put(KD, n, 0, n, cols("w_in", 0, KD, c0, n)(L))
                    elif name == "u":
                        put(KD, 256, 0, 256, cols("w_in", 0, KD, U0 + 256 * i, 256)(L))
                    elif name == "gate":
                        put(KD, 256, 0, 256, cols("w_in", 0, KD, GA0 + 256 * i, 256)(L))
                    elif name == "w_a":
                        for g in range(KV):
                            w = A["w_a"].rearrange("l (g c d) n -> d (l g) c n", g=KV, c=4)
                            put(4, 512, 0, 512, w[:, ds(L * KV + g, 1), :, 512 * i:512 * i + 512]
                                .rearrange("d a c n -> d (a c) n"), slice(64 * g, 64 * g + 64))
                    elif name == "glu":
                        put(4, 256, 0, 512, cols("w_glu1", 0, 4, 256 * i, 256)(L))
                        put(4, 256, 256, 512, cols("w_glu2", 0, 4, 256 * i, 256)(L))
                    elif name == "w_o":
                        put(KD, 256, 0, 256, cols("w_o", 0, KD, 256 * i, 256)(L))
                    elif name == "up":
                        put(KD, P, 0, 256, cols("w_up", 0, KD, P * i, P)(L))
                        put(KD, P, P, 256, cols("w_up", 0, KD, FF + P * i, P)(L))
                    elif name == "down":
                        put(11, P, 0, P, cols("w_down", 11 * (i % 2), 11, P * (i // 2), P)(L))
                    elif name == "ple":
                        put(2, D, 0, D, cols("w_ple", 0, 2, 0, D)(L))
                    elif name == "ple_gate":
                        put(KD, 256, 0, 256, cols("w_ple_gate", 0, KD, 256 * i, 256)(L))

        def dmas_of(name):
            return 2 if name in ("cmp", "w_a", "glu", "up") else 1

        slot_total = [sum(16 * dmas_of(n) for n, _ in CHUNKS[s::SLOTS]) for s in range(SLOTS)]

        def slot_count(m):
            return sum(16 * dmas_of(n) for n, _ in CHUNKS[m % SLOTS:m + 1:SLOTS])

        @block.gpsimd
        def _(pool):
            def await_(what, count):
                count = pool.to_reg(count)
                pool.wait_ge(consts_in, 16 * CONSTS)
                pool.wait_ge(what, count)

            with nc.allow_non_contiguous_dma(reason="short rows"):
                pool.dma_start(xrows[:, 0:2, :], A["x_prompt"].rearrange("b (t p) d -> p (b t) d", p=P)).then_inc(x_in, 16)
                pool.dma_start(xrows[0:NB, 2, :], A["x_sample"].rearrange("s a d -> s (a d)")).then_inc(x_in, 16)
                pool.memset(qpad[:], 0.0).then_inc(zeroed, 1)
                pool.memset(GX[:, :, 0:2], 0.0).then_inc(zeroed, 1)
                with pool.Fori(0, DEPTH) as L:
                    pool.sem_clear(pool_step)
                    step = [0]

                    def link(ins):
                        step[0] += 1
                        ins.then_inc(pool_step, 1)
                        pool.wait_ge(pool_step, step[0])

                    def load(dst, src, done):
                        pool.dma_start(dst, src).then_inc(done, 16)

                    def layer(name, how, **kw):
                        return A[name].rearrange(how, **kw)

                    for j, g in enumerate(("g_attn", "g_ffn", "g_ple")):
                        load(prm_rows[KD * j:KD * j + KD, :], A[g].rearrange("l (k p) -> (l k) p", p=P)[ds(L * KD, KD), :], params_in)
                    load(prm_rows[24:28, :], A["ssm_d"].rearrange("l (k g) c -> (l k) (g c)", g=8)[ds(L * 4, 4), :], params_in)
                    load(ssm_rows[:, 0, :], A["ssm_a_re"].rearrange("l (i g) s -> (l i) (g s)", g=2)[ds(L * ST, ST), :], params_in)
                    load(ssm_rows[:, 1, :], A["ssm_a_im"].rearrange("l (i g) s -> (l i) (g s)", g=2)[ds(L * ST, ST), :], params_in)
                    load(dt_rows[:], A["ssm_log_dt"].rearrange("l (i g) -> (l i) g", g=2)[ds(L * ST, ST), :], params_in)
                    for j, g in enumerate(("g_q", "g_kc", "g_ks", "g_kw")):
                        load(gains[:, j, :], A[g][ds(L, 1), :].broadcast_to([P, HD]), more_in)
                    load(w2[:, 0, :], A["cmp_wk2"].rearrange("l f d -> (l f) d")[ds(L * P, P), :], more_in)
                    load(w2[:, 1, 0:32], A["cmp_wk2"].rearrange("l f d -> (l f) d")[ds(L * P, P), 32:64], more_in)
                    load(w2[:, 1, 32:64], A["cmp_wk2"].rearrange("l f d -> (l f) d")[ds(L * P, P), 0:32], more_in)
                    load(w2[:, 2, :], A["cmp_wv2"].rearrange("l f d -> (l f) d")[ds(L * P, P), :], more_in)
                    load(pe_rows[:, 0, :], A["cmp_pek"].rearrange("l (j a) d -> (l j) (a d)", a=2)[ds(L * 16, 16), :], pe_in)
                    load(pe_rows[:, 1, :], A["cmp_pev"].rearrange("l (j a) d -> (l j) (a d)", a=2)[ds(L * 16, 16), :], pe_in)
                    load(h0_rows[:, 0, :], A["state_ssm_re"].rearrange("l s (i g) n -> (l s i) (g n)", g=2)[ds(L * P, P), :], h0_in)
                    load(h0_rows[:, 1, :], A["state_ssm_im"].rearrange("l s (i g) n -> (l s i) (g n)", g=2)[ds(L * P, P), :], h0_in)

                    await_(h_done, L * KD + KD)
                    sel_pool = A["cache_sel"].rearrange("l n t v g d -> t (l n) v (g d)")
                    cmp_pool = A["cache_cmp"].rearrange("l n (t a) v g d -> t (l n) a (v g) d", a=2)
                    n_pool = A["cache_sel"].shape[1]
                    def turn(src, k, i, ni, n, outs):
                        cc, sn = (cs[:, j, k, i:i + ni].unsqueeze(1).unsqueeze(3).broadcast_to([P, 2, ni, n]) for j in range(2))
                        w0, w1 = (rotw[:, j, 0:2 * ni * n].rearrange("p (c i t) -> p c i t", c=2, i=ni) for j in range(2))
                        pool.tensor_tensor(w0, src, cc, ALU.mult)
                        link(pool.tensor_tensor(w1, src, sn, ALU.mult))
                        pool.tensor_tensor(outs[0], w0[:, 0], w1[:, 1], ALU.subtract)
                        return pool.tensor_tensor(outs[1], w0[:, 1], w1[:, 0], ALU.add)

                    def small_tables():
                        await_(trig_ready, L + 1)
                        pool.memset(rot0[:, 0, :, 0:1], 1.0)
                        link(pool.memset(rot0[:, 1, :, 0:1], 0.0))
                        for k in range(5):
                            n = 1 << k
                            link(turn(rot0[:, :, :, 0:n], k, 0, ST, n, [rot0[:, c, :, n:2 * n] for c in range(2)]))

                    def tables(q):
                        if q >= 2:
                            await_(rot_used, L * (ST // 2) + (q - 1))
                        if q >= 1:
                            await_(rot_ready, L * (ST // 2) + q)
                        T = rot[:, q % 2]
                        pool.tensor_tensor(T[:, :, :, 0:32], rot0[:, :, 2 * q:2 * q + 2, :],
                                           c_ones[:, 0:1].unsqueeze(1).unsqueeze(1).broadcast_to([P, 2, 2, 32]), ALU.mult)
                        for k in range(5, 8):
                            n = 1 << k
                            src = rot0[:, :, 2 * q:2 * q + 2, :] if k == 5 else T[:, :, :, 0:n]
                            last = turn(src, k, 2 * q, 2, n, [T[:, c, :, n:2 * n] for c in range(2)])
                            if k < 7:
                                link(last)
                            else:
                                last.then_inc(rot_ready, 1)

                    for s in range(NB):
                        if s == 1:
                            small_tables()
                            tables(0)
                        if s >= 2:
                            await_(act_freed, caches_turned(L, s - 2))
                        for b in range(PAGES):
                            page = pool.value_load(pt_sb[0:1, s * PAGES + b:s * PAGES + b + 1], min_val=0, max_val=n_pool - 1)
                            load(kst[:, s % 2, 0, b, :], sel_pool[:, ds(L * n_pool + page, 1), 0, :].rearrange("t a k -> t (a k)"), k_in[s % 2])
                            for a in range(2):
                                load(cst[64 * b:64 * b + 64, s % 2, :].rearrange("p (w a d) -> p w a d", w=4, a=2)[:, :, a, :],
                                     cmp_pool[:, ds(L * n_pool + page, 1), a, :, :].rearrange("t l w d -> t (l w) d"), cmp_in[s % 2])
                        if s > 0:
                            tables(s)
                    await_(rot_used, L * (ST // 2) + ST // 2)
                    for s in range(NB):
                        for b in range(PAGES):
                            page = pool.value_load(pt_sb[0:1, s * PAGES + b:s * PAGES + b + 1], min_val=0, max_val=n_pool - 1)
                            load(vpast[:, 0, s, b, :], sel_pool[:, ds(L * n_pool + page, 1), 1, :].rearrange("t a k -> t (a k)"), v_in)
                    win_v = A["cache_win"].rearrange("l s (b t) v g d -> t (l s b) v (g d)", b=PAGES)
                    for s in range(0, NB, NB // 2):
                        load(vpast[:, 1, s:s + NB // 2].rearrange("p s b k -> p (s b) k"),
                             win_v[:, ds(L * NB * PAGES + s * PAGES, NB // 2 * PAGES), 1, :], v_in)
                    pool.dma_start(win_s.rearrange("l s t v g d -> (l s) (t v g d)")[ds(L * NB, NB), 0:(PAST - 1) * 256],
                                   A["cache_win"].rearrange("l s t v g d -> (l s) (t v g d)")[ds(L * NB, NB), 256:PAST * 256]).then_inc(copies_out, 16)
                    pool.dma_start(conv_s.rearrange("l s j f -> (l s) j f")[ds(L * NB, NB), 0, :],
                                   A["state_conv"].rearrange("l s j f -> (l s) j f")[ds(L * NB, NB), 1, :]).then_inc(copies_out, 16)

                    await_(act_freed, act_jobs(L, "states", 1))
                    for j, (o_p, o_s) in enumerate(((re_p, re_s), (im_p, im_s))):
                        pool.dma_start(o_s.rearrange("l s (i g) n -> (l s i) (g n)", g=2)[ds(L * P, P), :], st_out[:, j, :]).then_inc(states_out, 16)
                        pool.dma_start(o_p.rearrange("l b (i g) n -> (l b i) (g n)", g=2)[ds(L * ST, ST), :], fin_out[:, j, :]).then_inc(states_out, 16)
                    cmp_rows_out = cmp_p.rearrange("l b (t p) v g d -> p (l b t) (v g d)", p=P)
                    await_(roped, L * 3 + 2)
                    pool.dma_start(cmp_rows_out[:, ds(L * 2, 2), :], z[:, 0:2, QW:QW + 256]).then_inc(cmp_out, 16)
                    await_(cmp_out, L * 16 + 16)
                    for a in range(2):
                        load(prompt_cmp[:].rearrange("p (w a d) -> p w a d", w=4, a=2)[:, :, a, :],
                             cmp_p.rearrange("l b (t a) v g d -> (l b t) a (v g) d", a=2)[ds(L * P, P), a, :, :], rows_back)
                    await_(roped, L * 3 + 3)
                    for j, (outp, outs) in enumerate(((cmp_p, cmp_s), (sel_p, sel_s), (win_p, None))):
                        c0 = QW + 2 * KVW * j
                        if j > 0:
                            pool.dma_start(outp.rearrange("l b (t p) v g d -> p (l b t) (v g d)", p=P)[:, ds(L * 2, 2), :],
                                           z[:, 0:2, c0:c0 + 256]).then_inc(rows_out, 16)
                        if outs is not None:
                            pool.dma_start(outs.rearrange("l s a v g d -> (l s) (a v g d)")[ds(L * NB, NB), :],
                                           z[0:NB, 2, c0:c0 + 256]).then_inc(rows_out, 16)
                    pool.dma_start(win_s.rearrange("l s t v g d -> (l s) (t v g d)")[ds(L * NB, NB), (PAST - 1) * 256:PAST * 256],
                                   z[0:NB, 2, 1024:1280]).then_inc(rows_out, 16)

                    await_(o_ready, L * 5 + 1)
                    load(conv_rows[0:16, :], A["state_conv"].rearrange("l s j f -> (l s j) f")[ds(L * 16, 16), :], conv_in)
                    load(conv_rows[16:19, :], A["conv_w"].rearrange("l j f -> (l j) f")[ds(L * 3, 3), :], conv_in)
                    load(conv_rows[19:20, :], A["conv_b"][ds(L, 1), :], conv_in)
                    await_(dve_freed, dve_jobs(L, "w_o", 1))
                    load(p_rows[:, 0:2, :], A["p_prompt"].rearrange("l b (t p) k -> p (l b t) k", p=P)[:, ds(L * 2, 2), :], ple_in)
                    load(p_rows[0:NB, 2, :], A["p_sample"].rearrange("l s a k -> (l s) (a k)")[ds(L * NB, NB), :], ple_in)
                    await_(act_freed, act_jobs(L, "gate_rows", 6))
                    pool.dma_start(conv_p.rearrange("l b j f -> (l b j) f")[ds(L * 2, 2), :], gp_rows[0:2, :]).then_inc(conv_out, 16)
                    pool.dma_start(conv_s.rearrange("l s j f -> (l s) j f")[ds(L * NB, NB), 1, :], gp_rows[2:10, :]).then_inc(conv_out, 16)
                    await_(conv_out, L * 32 + 32)
                    await_(states_out, L * 64 + 64)
                await_(act_freed, act_jobs(DEPTH, "u", 3))
                await_(dve_freed, dve_jobs(DEPTH, "params", 3))
                pool.dma_start(y_prompt.rearrange("b (t p) d -> p (b t) d", p=P), xrows[:, 0:2, :]).then_inc(y_out, 16)
                pool.dma_start(y_sample.rearrange("s a d -> s (a d)"), xrows[0:NB, 2, :]).then_inc(y_out, 16)
                pool.wait_ge(copies_out, DEPTH * 32)
                await_(rows_out, DEPTH * 80)
                await_(cmp_out, DEPTH * 16)
                await_(states_out, DEPTH * 64)
                await_(conv_out, DEPTH * 32)
                pool.wait_ge(y_out, 32)

        @block.tensor
        def _(pe):
            def small():
                pe.wait_ge(consts_in, 16 * CONSTS)

            def run(L, program, base_a, base_v):
                n_a, n_v, chunk = [0], [0], [0]

                def act_bank(few_rows=False):
                    n = n_a[0]
                    n_a[0] += 1
                    if n >= BANKS or base_a is not None:
                        count = (base_a if base_a is not None else 0) + (n - BANKS + 1 if n >= BANKS else 0)
                        if few_rows:
                            count = pe.to_reg(count)
                            small()
                        pe.wait_ge(act_freed, count)
                    return bankA[n % BANKS]

                def dve_bank(few_rows=False):
                    n = n_v[0]
                    n_v[0] += 1
                    if n >= BANKS or base_v is not None:
                        count = (base_v if base_v is not None else 0) + (n - BANKS + 1 if n >= BANKS else 0)
                        if few_rows:
                            count = pe.to_reg(count)
                            small()
                        pe.wait_ge(dve_freed, count)
                    return bankV[n % BANKS]

                def next_chunk():
                    m = chunk[0]
                    chunk[0] += 1
                    pe.wait_ge(weights_in[m % SLOTS], L * slot_total[m % SLOTS] + slot_count(m))
                    fresh[0] = True
                    return ring[:, m % SLOTS, :]

                fresh = [False]

                def mm(out, lhsT, rhs, k, nk):
                    ins = pe.matmul(out, lhsT, rhs, start=(k == 0), stop=(k == nk - 1))
                    if fresh[0]:
                        assert k < nk - 1
                        ins.then_inc(weights_used, 1)
                        fresh[0] = False
                    return ins

                program(L, act_bank, dve_bank, next_chunk, mm)
                return n_a[0], n_v[0], chunk[0]

            def prologue(L, act_bank, dve_bank, next_chunk, mm):
                pe.wait_ge(ident_in, 16)
                pe.wait_ge(x_in, 32)
                for k in range(KD):
                    bank = act_bank() if k % 2 == 0 else dve_bank()
                    for t in range(2):
                        pe.transpose(bank[:, t * P:t * P + P], xrows[:, t, k * P:k * P + P], ident)
                    pe.transpose(bank[:, SEQ:NT], xrows[0:NB, 2, k * P:k * P + P], ident[0:NB, 0:NB]).then_inc(act_ready if k % 2 == 0 else dve_ready, 1)

            def layer(L, act_bank, dve_bank, next_chunk, mm):
                small()
                pe.wait_ge(params_in, L * 112 + 112)
                pe.wait_ge(dt_rows_ready, L + 1)
                bank = dve_bank(few_rows=True)
                pe.transpose(bank[:, 0:28], prm_rows[:], ident[0:28, 0:28])
                for j in range(3):
                    last = pe.transpose(bank[:, 28 + ST * j:28 + ST * j + ST], ssm_rows[:, j, :], ident[0:ST, 0:ST])
                last.then_inc(dve_ready, 1)
                def cmp_rows(rows):
                    bank = act_bank()
                    for c in range(0, 4 * P, P):
                        last = pe.transpose(bank[:, c:c + P], rows[:, c:c + P], ident)
                    last.then_inc(act_ready, 1)

                def cache_rows(j):
                    s, what = divmod(j, 2)
                    if what == 0:
                        pe.wait_ge(k_in[s % 2], L * 2 * 16 * (NB // 2) + 2 * 16 * (s // 2 + 1))
                        pe.wait_ge(kw_in[s % 2], L * 16 * (NB // 2) + 16 * (s // 2 + 1))
                        bank = act_bank()
                        for b in range(2):
                            for g in range(PAGES):
                                c = (2 * b + g) * P
                                last = pe.transpose(bank[:, c:c + P], kst[:, s % 2, b, g, :], ident)
                        last.then_inc(act_ready, 1)
                    else:
                        pe.wait_ge(cmp_in[s % 2], L * 4 * 16 * (NB // 2) + 4 * 16 * (s // 2 + 1))
                        cmp_rows(cst[:, s % 2, :])

                def sum_squares(n):
                    bank = dve_bank()
                    if n == 0:
                        for k in range(KD):
                            pe.wait_ge(squared, L * 3 * KD + k + 1)
                            last = mm(bank[:, 0:NT], c_ones[:], xn[:, k, :], k, KD)
                    else:
                        pe.wait_ge(added, L * 2 + n)
                        last = pe.matmul(bank[:, 0:NT], c_ones[:], xn[:, KD - 1, :], start=True, stop=True)
                    last.then_inc(dve_ready, 1)

                sum_squares(0)

                def normed_to(n, k):
                    pe.wait_ge(normed, L * 3 * KD + (n * KD + k + 1))

                def columns(width, tiles, rhs, nk, claim, ready, norm=None):
                    w = next_chunk()[:, 0:nk * width].rearrange("p (k n) -> p k n", k=nk)
                    for j in range(tiles):
                        bank = claim()
                        for k in range(nk):
                            if norm is not None and j == 0:
                                normed_to(norm, k)
                            last = mm(bank[:, 0:NT], w[:, k, P * j:P * j + P], rhs[:, k, :], k, nk)
                        last.then_inc(ready, 1)

                for i in range(2):
                    columns(256, 2, xn, KD, act_bank, act_ready, 0 if i == 0 else None)

                pe.wait_ge(c_ready, L + 1)
                for r in range(2):
                    bank = dve_bank()
                    for k in range(4):
                        last = pe.transpose(bank[:, P * k:P * k + P], cpad[:, r, k].rearrange("p g s -> p (g s)"), ident)
                    last.then_inc(dve_ready, 1)
                pe.wait_ge(b_ready, L + 1)
                for r in range(2):
                    bank = dve_bank()
                    for k in range(4):
                        last = pe.transpose(bank[:, P * k:P * k + P], bpad[:, r, 4 * k:4 * k + 4].rearrange("p i g c -> p (i g c)"), ident)
                    last.then_inc(dve_ready, 1)

                pe.wait_ge(h0_in, L * 32 + 32)
                bank = dve_bank()
                for j in range(2):
                    last = pe.transpose(bank[:, P * j:P * j + P], h0_rows[:, j, :], ident)
                last.then_inc(dve_ready, 1)
                pe.wait_ge(dve_freed, dve_jobs(L, "b", 2))
                pe.wait_ge(u_spread, L + 1)
                bank = dve_bank()
                for k in range(4):
                    for r in range(2):
                        last = pe.matmul(bank[:, P * (4 * r + k) // 4:P * (4 * r + k + 1) // 4], BT[:, r, k, :],
                                         upad[:, k].rearrange("p j s -> p (j s)"), start=True, stop=True)
                last.then_inc(dve_ready, 1)

                def drive(i):
                    a, k = 32 * (i % 4), i // 4
                    bank = dve_bank()
                    for r in range(2):
                        last = pe.matmul(bank[:, SEQ * r:SEQ * r + SEQ], BT[a:a + 32, r, k, :], uT[a:a + 32, k, 0:SEQ],
                                         start=True, stop=True)
                    last.then_inc(dve_ready, 1)

                def outputs(i):
                    a, k = 32 * (i % 4), i // 4
                    pe.wait_ge(state_ready, L * ST + i + 1)
                    if i % 4 == 0:
                        pe.wait_ge(y_taken, L * 4 + k + 1)
                    o = bankY[a:a + 32, :]
                    for r in range(2):
                        pe.matmul(o[:, 0:SEQ], CT[:, r, k, a:a + 32], HH[:, i % 2, r, :], start=(r == 0), stop=(r == 1))
                    for r in range(2):
                        last = pe.matmul(o[:, SEQ:NT], CT[:, r, k, a:a + 32], hs[:, r, i:i + ST * (NB - 1) + 1:ST],
                                         start=(r == 0), stop=(r == 1))
                    last.then_inc(y_ready, 1)

                drive(0)

                gate_tile = [0]

                def gates(tiles):
                    for _ in range(tiles):
                        i = gate_tile[0]
                        gate_tile[0] += 1
                        if i % 2 == 0:
                            gate_w[0] = next_chunk()[:, 0:KD * 256].rearrange("p (k n) -> p k n", k=KD)
                        bank = act_bank()
                        for k in range(KD):
                            last = mm(bank[:, 0:NT], gate_w[0][:, k, P * (i % 2):P * (i % 2) + P], xn[:, k, :], k, KD)
                        last.then_inc(act_ready, 1)

                gate_w = [None]
                jobs = 0
                for c0, n in QW_CHUNKS:
                    w = next_chunk()[:, 0:KD * n].rearrange("p (k n) -> p k n", k=KD)
                    for t in range(3):
                        m = P if t < 2 else NB
                        bank = act_bank()
                        for k in range(KD):
                            last = mm(bank[0:m, 0:n], xn[:, k, P * t:P * t + m], w[:, k, :], k, KD)
                        last.then_inc(act_ready, 1)
                        cache_rows(jobs)
                        drive(jobs + 1)
                        outputs(jobs)
                        if jobs in GATES_AT:
                            gates(2)
                        jobs += 1
                cache_rows(jobs)
                outputs(jobs)
                small()
                pe.wait_ge(pe_in, L * 32 + 32)
                bank = act_bank(few_rows=True)
                for v in range(2):
                    last = pe.transpose(bank[:, 16 * v:16 * v + 16], pe_rows[:, v, :], ident[0:16, 0:16])
                last.then_inc(act_ready, 1)


                pe.wait_ge(state_ready, L * ST + ST)
                bank = act_bank()
                for r in range(2):
                    pe.transpose(bank[:, P * r:P * r + P], hs[:, r, :], ident)
                for r in range(2):
                    last = pe.transpose(bank[0:ST, 256 + P * r:256 + P * r + P], hfin[:, r, :], ident)
                last.then_inc(act_ready, 1)

                gates(4)

                for t in range(3):
                    small()
                    pe.wait_ge(roped, L * 3 + t + 1)
                    m = P if t < 2 else NB
                    eye = ident[0:m, 0:m]
                    bank = act_bank(few_rows=True)
                    for c in range(4):
                        last = pe.transpose(bank[:, m * c:m * c + m], z[0:m, t, KVW * c:KVW * c + KVW], eye)
                    if t < 2:
                        last.then_inc(act_ready, 1)
                        small()
                        bank = act_bank(few_rows=True)
                    off = 0 if t < 2 else 4 * NB
                    for j, c0 in enumerate((768, 1024)):
                        last = pe.transpose(bank[:, off + m * j:off + m * j + m], z[0:m, t, c0:c0 + KVW], eye)
                    last.then_inc(act_ready, 1)
                    if t < 2:
                        gates(2)
                bank = dve_bank()
                pe.wait_ge(gates_ready, L + 1)
                pe.matmul(bank[0:64, 0:24], c_sel[:], bg[0:NB, 2, :], start=True, stop=True).then_inc(dve_ready, 1)

                pe.wait_ge(rows_back, L * 32 + 32)
                cmp_rows(prompt_cmp[:])
                pe.wait_ge(act_freed, act_jobs(L, "hidden"))
                for v in range(2):
                    w = next_chunk()[:, 0:16 * P].rearrange("p (j f) -> p j f", j=16)
                    bank = act_bank()
                    for j in range(16):
                        last = mm(bank[:, 0:XR * NCMP], w[:, j, :], XT[:, v, :, j:j + 8 * NCMP - 7:8], j, 16)
                    last.then_inc(act_ready, 1)
                pe.wait_ge(act_freed, act_jobs(L, "hidden", 1))
                bank = dve_bank()
                pe.wait_ge(more_in, L * 128 + 128)
                n = NSEQ * NCMP
                for r in range(2):
                    for g in range(KV):
                        last = pe.matmul(bank[64 * g:64 * g + 64, 256 * r:256 * r + n], w2[:, r, :], hg[:, 0, n * g:n * g + n],
                                         start=True, stop=True)
                last.then_inc(dve_ready, 1)
                pe.wait_ge(act_freed, act_jobs(L, "hidden", 2))
                for j in range(3):
                    bank = act_bank()
                    for i in range(3):
                        for g in range(KV):
                            c = (g * NSEQ + 3 * j + i) * NCMP
                            last = pe.matmul(bank[0:NCMP, (2 * i + g) * HD:(2 * i + g + 1) * HD], hg[:, 1, c:c + NCMP], w2[:, 2, :],
                                             start=True, stop=True)
                    last.then_inc(act_ready, 1)

                pe.wait_ge(kcmp_ready, L + 1)
                pe.wait_ge(act_freed, act_jobs(L, "v_cmp", 3))
                for c0, n in ((0, 2 * PAST), (NEW0, KEYS - NEW0)):
                    bank = dve_bank()
                    for s in range(NB):
                        last = mm(bank[0:64, 0:n], qpad[:, 64 * s:64 * s + 64], keys[:, s, c0:c0 + n], s, NB)
                    last.then_inc(dve_ready, 1)

                for g in range(KV):
                    bank = dve_bank()
                    for t in range(2):
                        for c in range(4):
                            last = pe.matmul(bank[:, NCMP * (4 * t + c):NCMP * (4 * t + c + 1)], qT[64 * g:64 * g + 64, c, P * t:P * t + P],
                                             kcmp[64 * g:64 * g + 64, :], start=True, stop=True)
                    last.then_inc(dve_ready, 1)

                def head_scores(u):
                    idx, t = divmod(u, 2)
                    c, g = divmod(idx, 2)
                    bank = dve_bank()
                    n = P * (t + 1)
                    pe.matmul(bank[:, 0:2 * n], qT[64 * g:64 * g + 64, c, P * t:P * t + P], kT[64 * g:64 * g + 64, :, 0:n],
                              start=True, stop=True).then_inc(dve_ready, 1)

                head_scores(0)
                gates(2)

                small()
                pe.wait_ge(s_prob, L + 1)
                bank = act_bank(few_rows=True)
                for b in range(4):
                    pe.transpose(bank[:, 64 * b:64 * b + 64], SS[:, P * b:P * b + P], ident[0:64, 0:64])
                pe.transpose(bank[0:NCMP, 256:320], SS[:, CMP0:KEYS], ident[0:64, 0:64])
                for b in range(2):
                    last = pe.transpose(bank[0:NB, 320 + 64 * b:384 + 64 * b], snew[:, b, :], ident[0:64, 0:64])
                last.then_inc(act_ready, 1)
                head_scores(1)
                pe.wait_ge(v_in, L * V_LOADS + V_LOADS)
                pe.wait_ge(act_freed, act_jobs(L, "s_probs", 1))
                pe.wait_ge(o_taken, L * 5 + 1)
                for b, c0 in enumerate((896, 1152)):
                    pe.matmul(bankO[:, 0:64], z[0:NB, 2, c0:c0 + KVW], PTs[0:NB, 320 + 64 * b:384 + 64 * b],
                              start=(b == 0), stop=False, skip_group_check=True)
                for s in range(NB):
                    o = bankO[:, 8 * s:8 * s + 8]
                    for b in range(2):
                        for g in range(PAGES):
                            c = 64 * (2 * b + g) + 8 * s
                            pe.matmul(o, vpast[:, b, s, g, :], PTs[:, c:c + 8], start=False, stop=False, skip_group_check=True)
                    last = pe.matmul(o, vcmp[:, s, :], PTs[0:NCMP, 256 + 8 * s:264 + 8 * s], start=False, stop=(s == NB - 1),
                                     skip_group_check=True)
                last.then_inc(o_ready, 1)

                pe.wait_ge(c_prob, L + 1)
                head_scores(2)

                def turn_cmp(c):
                    bank = act_bank()
                    for g in range(KV):
                        for t in range(2):
                            last = pe.transpose(bank[0:NCMP, (2 * g + t) * P:(2 * g + t + 1) * P], SP_[:, 8 * t + 4 * g + c, :], ident)
                    last.then_inc(act_ready, 1)

                def turn_probs(u):
                    t = u % 2
                    pe.wait_ge(p_prob, L * 16 + u + 1)
                    bank = act_bank()
                    for b in range(2):
                        for k in range(t + 1):
                            c = ((t + 1) * b + k) * P
                            last = pe.transpose(bank[:, c:c + P], S(u)[:, b, P * k:P * k + P], ident)
                    last.then_inc(act_ready, 1)

                def head_out(idx):
                    c, g = divmod(idx, 2)
                    pe.wait_ge(act_freed, probs_turned(L, 2 * idx + 1))
                    if g == 0:
                        pe.wait_ge(o_taken, L * 5 + 1 + c + 1)
                    o = bankO[64 * g:64 * g + 64, :]
                    vc = (896, 1152)
                    pe.matmul(o[:, 0:SEQ], vcmp[:, NB, HD * g:HD * g + HD], pcw[0:NCMP, c % 2, 2 * P * g:2 * P * g + 2 * P],
                              start=True, stop=False, skip_group_check=True)
                    for b in range(2):
                        pe.matmul(o[:, 0:SEQ], z[:, 0, vc[b] + HD * g:vc[b] + HD * g + HD], PT[:, idx % 2, b, 0, :],
                                  start=False, stop=False, skip_group_check=True)
                    for b in range(2):
                        last = pe.matmul(o[:, P:SEQ], z[:, 1, vc[b] + HD * g:vc[b] + HD * g + HD], PT[:, idx % 2, b, 1, P:SEQ],
                                         start=False, stop=(b == 1), skip_group_check=True)
                    if g == 1:
                        last.then_inc(o_ready, 1)

                for u in range(2 * H):
                    if u + 3 < 2 * H:
                        head_scores(u + 3)
                    if u % 4 == 0:
                        turn_cmp(u // 4)
                    turn_probs(u)
                    if u % 2 == 0 and u >= 2:
                        head_out(u // 2 - 1)
                head_out(H - 1)

                pe.wait_ge(o_taken, L * 5 + 6)
                for i in range(2):
                    columns(512, 4, aT, 4, dve_bank, dve_ready)
                pe.wait_ge(y_gelu, L * 4 + 4)
                for i in range(4):
                    w = next_chunk()[:, 0:4 * 512].rearrange("p (k n) -> p k n", k=4)
                    for j in range(2):
                        for half, claim, ready in ((1, act_bank, act_ready), (0, dve_bank, dve_ready)):
                            bank = claim()
                            for k in range(4):
                                c = 256 * half + P * j
                                last = mm(bank[:, 0:NT], w[:, k, c:c + P], uT[:, k, :], k, 4)
                            last.then_inc(ready, 1)
                pe.wait_ge(merged, L * KD + KD)
                for i in range(4):
                    columns(256, 2, sg[:, 0], KD, dve_bank, dve_ready)

                small()
                pe.wait_ge(conv_in, L * 48 + 48)
                bank = act_bank(few_rows=True)
                for f in range(KF):
                    last = pe.transpose(bank[:, 20 * f:20 * f + 20], conv_rows[:, P * f:P * f + P], ident[0:20, 0:20])
                last.then_inc(act_ready, 1)
                sum_squares(1)
                for f in range(KF):
                    w = next_chunk()[:, 0:KD * 256].rearrange("p (k n) -> p k n", k=KD)
                    for half, claim, ready in ((0, act_bank, act_ready), (1, dve_bank, dve_ready)):
                        bank = claim()
                        for k in range(KD):
                            if f == 0 and half == 0:
                                normed_to(1, k)
                            last = mm(bank[:, 0:NT], w[:, k, P * half:P * half + P], xn[:, k, :], k, KD)
                        last.then_inc(ready, 1)
                pe.wait_ge(act_freed, act_jobs(L, "up", KF))
                for j in range(6):
                    bank = act_bank()
                    for f in range(4 * j, min(4 * j + 4, KF)):
                        last = pe.transpose(bank[0:10, P * (f - 4 * j):P * (f - 4 * j) + P], gcol[:, f, :], ident)
                    last.then_inc(act_ready, 1)
                for o in range(KD):
                    bank = dve_bank()
                    for half in range(2):
                        w = next_chunk()[:, 0:11 * P].rearrange("p (k n) -> p k n", k=11)
                        for k in range(11):
                            kk = 11 * half + k
                            pe.wait_ge(dve_freed, dve_jobs(L, "up", kk + 1)) if o == 0 else None
                            last = mm(bank[:, 0:NT], w[:, k, :], act[:, kk, :], kk, KF)
                    last.then_inc(dve_ready, 1)

                pe.wait_ge(ple_in, L * 32 + 32)
                for k in range(2):
                    small()
                    bank = act_bank(few_rows=True)
                    for t in range(2):
                        pe.transpose(bank[:, P * t:P * t + P], p_rows[:, t, P * k:P * k + P], ident)
                    pe.transpose(bank[:, SEQ:NT], p_rows[0:NB, 2, P * k:P * k + P], ident[0:NB, 0:NB]).then_inc(act_ready, 1)
                pe.wait_ge(act_freed, act_jobs(L, "ple_in", 2))
                sum_squares(2)
                columns(D, KD, pT, 2, act_bank, act_ready)
                for i in range(4):
                    columns(256, 2, xn, KD, act_bank, act_ready, 2 if i == 0 else None)

            def epilogue(L, act_bank, dve_bank, next_chunk, mm):
                pe.wait_ge(h_done, DEPTH * KD + KD)
                for t in range(3):
                    m = P if t < 2 else NB
                    for j in range(2):
                        bank = act_bank() if j == 0 else dve_bank()
                        for k in range(4):
                            last = pe.transpose(bank[0:m, P * k:P * k + P], hT[:, 4 * j + k, P * t:P * t + m], ident)
                        last.then_inc(act_ready if j == 0 else dve_ready, 1)

            pe.sem_inc(weights_used, SLOTS)
            assert run(0, prologue, None, None)[0:2] == (ACT_PRO, DVE_PRO)
            with pe.Fori(0, DEPTH) as L:
                counts = run(L, layer, L * ACT_LAYER + ACT_PRO, L * DVE_LAYER + DVE_PRO)
            assert counts == (ACT_LAYER, DVE_LAYER, NCH), counts
            run(DEPTH, epilogue, DEPTH * ACT_LAYER + ACT_PRO, DEPTH * DVE_LAYER + DVE_PRO)

        @block.scalar
        def _(act_):
            n = [0]

            def fn(out, in_, func=ACT.Copy, **kw):
                return act_.activation(out, in_, func, **kw)

            def take(base):
                act_.wait_ge(act_ready, base + (n[0] + 1))
                n[0] += 1
                return bankA[(n[0] - 1) % BANKS]

            act_.sem_inc(o_taken, 1)
            for k in range(0, KD, 2):
                fn(hT[:, k, :], take(0)[:, 0:NT]).then_inc(act_freed, 1)

            def squares(L, i, done, at, tiles=range(KD)):
                for k in tiles:
                    act_.wait_ge(done, at(k))
                    fn(xn[:, k, :], hT[:, k, :], ACT.Square).then_inc(squared, 1)

            def std(L, i):
                fn(warm[:], c_bias[:, 1:2], ACT.Sqrt)
                act_.wait_ge(dve_ready, dve_jobs(L, f"norm{i}", 1))
                fn(rstd[:], bankV[V_AT[f"norm{i}"] % BANKS][:, 0:NT], ACT.Sqrt, scale=1.0 / D, bias=c_bias[:, 0:1]).then_inc(std_ready, 1)

            act_.wait_ge(consts_in, 16 * CONSTS)
            act_.wait_ge(zeroed, 2)
            with act_.Fori(0, DEPTH) as L:
                n[0] = 0
                base = L * ACT_LAYER + ACT_PRO
                squares(L, 0, h_done, lambda k: L * KD + (k + 1))
                with nc.allow_non_contiguous_dma(reason="short rows"):
                    act_.dma_start(bst[:, 0], A["ssm_b_re"].rearrange("l (i g) s c -> (g s) (l i) c", g=2)[:, ds(L * ST, ST), :]).then_inc(smat_in, 16)
                    act_.dma_start(bst[:, 1], A["ssm_b_im"].rearrange("l (i g) s c -> (g s) (l i) c", g=2)[:, ds(L * ST, ST), :]).then_inc(smat_in, 16)
                    act_.dma_start(cst_c[:, 0], A["ssm_c_re"].rearrange("l (k g) c s -> (g c) (l k) s", g=8)[:, ds(L * 4, 4), :]).then_inc(smat_in, 16)
                    act_.dma_start(cst_c[:, 1], A["ssm_c_im"].rearrange("l (k g) c s -> (g c) (l k) s", g=8)[:, ds(L * 4, 4), :]).then_inc(smat_in, 16)
                act_.wait_ge(dve_freed, dve_jobs(L, "params", 1))
                fn(sm[:, 0, :], prm[:, 28 + 2 * ST:28 + 3 * ST], ACT.Exp).then_inc(dt_ready, 1)
                act_.wait_ge(trig_arg, L + 1)
                fn(sm[:, 3, :], sm[:, 2, :], ACT.Exp)
                fn(cs[:, 0], ang[:, 2], ACT.Sin, scale=-1.0, bias=c_bias[:, 1:2])
                fn(cs[:, 1], ang[:, 0], ACT.Sin).then_inc(trig_ready, 1)
                std(L, 0)

                def cache_rows(j):
                    s, what = divmod(j, 2)
                    bank = take(base)
                    if what == 0:
                        fn(keys[:, s, 0:2 * PAST], bank[:]).then_inc(act_freed, 1)
                        if s + 2 < NB:
                            window_keys(s + 2)
                    else:
                        fn(XT[:, :, 0:2 * NSEQ, :].rearrange("p v (g s) t -> p v g s t", g=KV)[:, :, :, s, :],
                           bank[:].rearrange("p (v g t) -> p v g t", v=2, g=KV)).then_inc(act_freed, 1)

                win = A["cache_win"].rearrange("l s (b t) v g d -> t (l s) b v (g d)", b=PAGES)

                def window_keys(s):
                    act_.dma_start(kst[:, s % 2, 1, :, :], win[:, ds(L * NB + s, 1), :, 0, :]
                                   .rearrange("t a b k -> t (a b) k")).then_inc(kw_in[s % 2], 16)

                for s in range(2):
                    window_keys(s)

                gate_tile = [0]

                def gates(tiles):
                    for _ in range(tiles):
                        i = gate_tile[0]
                        gate_tile[0] += 1
                        fn(sg[:, i // KD, i % KD, :], take(base)[:, 0:NT], ACT.Tanh, scale=0.5).then_inc(act_freed, 1)

                for i in range(4):
                    fn(uT[:, i, :], take(base)[:, 0:NT]).then_inc(act_freed, 1)
                jobs = 0
                for c0, w in QW_CHUNKS:
                    for t in range(3):
                        m = P if t < 2 else NB
                        dst, src = z[0:m, t, c0:c0 + w], take(base)[0:m, 0:w]
                        if c0 < QW:
                            dst = z[0:m, t, 0:QW].rearrange("p (c g d) -> p c g d", c=4, g=KV)[:, :, c0 // 256, :]
                            src = src.rearrange("p (c d) -> p c d", c=4)
                        fn(dst, src).then_inc(act_freed, 1)
                        cache_rows(jobs)
                        if jobs in GATES_AT:
                            gates(2)
                        jobs += 1
                cache_rows(jobs)
                bank = take(base)
                for v in range(2):
                    last = fn(XT[:, v, 2 * NSEQ, :].rearrange("p (r j) -> p r j", j=16),
                              bank[:, 16 * v:16 * v + 16].unsqueeze(1).broadcast_to([P, 8, 16]))
                last.then_inc(act_freed, 1)
                act_.wait_ge(act_freed, act_jobs(L, "pe", 1))
                fn(bg[:, 0:2, :], z[:, 0:2, 1280:QKV], ACT.Tanh, scale=0.5)
                fn(bg[0:NB, 2, :], z[0:NB, 2, 1280:QKV], ACT.Tanh, scale=0.5).then_inc(gates_tanh, 1)
                bank = take(base)
                fn(st_out[:], bank[:, 0:2 * P].rearrange("p (r n) -> p r n", r=2))
                fn(fin_out[:], bank[0:ST, 2 * P:4 * P].rearrange("p (r n) -> p r n", r=2)).then_inc(act_freed, 1)

                gates(2)
                act_.wait_ge(hvar_ready, L + 1)
                fn(ss[:, 0:2, :], ss[:, 0:2, :], ACT.Sqrt)
                fn(ss[0:NB, 2, :], ss[0:NB, 2, :], ACT.Sqrt).then_inc(hstd_ready, 1)
                gates(2)
                for t in range(2):
                    fn(qT[:, :, P * t:P * t + P], take(base)[:].rearrange("p (c q) -> p c q", c=4)).then_inc(act_freed, 1)
                    fn(kT[:, :, P * t:P * t + P], take(base)[:, 0:2 * P].rearrange("p (b q) -> p b q", b=2)).then_inc(act_freed, 1)
                    gates(2)
                bank = take(base)
                for g in range(KV):
                    own = qpad[64 * g:64 * g + 64, :].rearrange("p (s x) -> p s x", s=NB)
                    fn(own[:, :, 4 * g:4 * g + 4], bank[64 * g:64 * g + 64, 0:4 * NB].rearrange("p (c s) -> p s c", c=4))
                fn(keys[:, :, NEW0:NEW0 + 2], bank[:, 4 * NB:6 * NB].rearrange("p (b s) -> p s b", b=2)).then_inc(act_freed, 1)
                fn(XT[:, :, 0:2 * NSEQ, :].rearrange("p v (g s) t -> p v g s t", g=KV)[:, :, :, NB, :],
                   take(base)[:].rearrange("p (v g t) -> p v g t", v=2, g=KV)).then_inc(act_freed, 1)
                for k in range(4):
                    act_.wait_ge(y_taken, L * 4 + k + 2)
                    fn(uT[:, k, :], uT[:, k, :], ACT.Gelu_apprx_tanh).then_inc(y_gelu, 1)
                for v in range(2):
                    bank = take(base)
                    fn(pe_col[:, v:v + 1], bank[:, 2 * NSEQ * NCMP:2 * NSEQ * NCMP + 1]).then_inc(pe_bias, 1)
                    act_.wait_ge(pe_bias, L * 2 + v + 1)
                    fn(hg[:, v, :], bank[:, 0:2 * NSEQ * NCMP], ACT.Gelu_apprx_tanh, bias=pe_col[:, v:v + 1]).then_inc(act_freed, 1)
                for j in range(3):
                    fn(vcmp[:, 3 * j:3 * j + 3, :], take(base)[0:NCMP, 0:3 * KVW].rearrange("p (s d) -> p s d", s=3)).then_inc(act_freed, 1)
                act_.wait_ge(s_max, L + 1)
                for b in range(2):
                    fn(SS[:, PAST * b:PAST * b + PAST], SS[:, PAST * b:PAST * b + PAST], ACT.Exp, bias=sq4[:, 4 + b:5 + b],
                       accum_out=sq4[:, 8 + b:9 + b])
                    fn(SS[:, NEW0 + b:NEW0 + b + 1], SS[:, NEW0 + b:NEW0 + b + 1], ACT.Exp, bias=sq4[:, 4 + b:5 + b])
                fn(SS[:, CMP0:KEYS], SS[:, CMP0:KEYS], ACT.Exp, bias=sq4[:, 6:7], accum_out=sq4[:, 10:11]).then_inc(s_exp, 1)
                gates(1)
                act_.wait_ge(c_arg, L + 1)
                fn(SP_, SP_, ACT.Exp).then_inc(c_exp, 1)
                gates(1)

                def exps(u):
                    act_.wait_ge(p_max, L * 2 * H + u + 1)
                    for b in range(2):
                        last = fn(S(u)[:, b], S(u)[:, b], ACT.Exp, bias=mx[:, u % 4, b:b + 1],
                                  accum_out=sums[:, u % 4, b:b + 1])
                    last.then_inc(p_exp, 1)

                exps(0)
                bank = take(base)
                fn(PTs[:, 0:256], bank[:, 0:256])
                fn(PTs[0:NCMP, 256:320], bank[0:NCMP, 256:320])
                fn(PTs[0:NB, 320:448], bank[0:NB, 320:448]).then_inc(act_freed, 1)
                exps(1)
                act_.wait_ge(o_ready, L * 5 + 1)
                for g in range(KV):
                    last = fn(aT[64 * g:64 * g + 64, :, SEQ:NT],
                              bankO[64 * g:64 * g + 64, 0:64].rearrange("p (s h) -> p h s", s=NB)[:, 4 * g:4 * g + 4, :])
                last.then_inc(o_taken, 1)
                for u in range(2 * H):
                    if u + 2 < 2 * H:
                        exps(u + 2)
                    if u % 4 == 0:
                        fn(pcw[0:NCMP, (u // 4) % 2, :], take(base)[0:NCMP, :]).then_inc(act_freed, 1)
                    t = u % 2
                    fn(PT[:, (u // 2) % 2, :, 0:t + 1, P * t:P * t + P],
                       take(base)[:, 0:2 * P * (t + 1)].rearrange("p (b k q) -> p b k q", b=2, k=t + 1)).then_inc(act_freed, 1)
                    if u % 4 == 0 and u >= 4:
                        c = u // 4 - 1
                        act_.wait_ge(o_ready, L * 5 + c + 2)
                        fn(aT[:, c, 0:SEQ], bankO[:, 0:SEQ]).then_inc(o_taken, 1)
                act_.wait_ge(o_ready, L * 5 + 5)
                fn(aT[:, 3, 0:SEQ], bankO[:, 0:SEQ]).then_inc(o_taken, 1)

                for o in range(KD):
                    if o >= 2:
                        act_.wait_ge(merged, L * KD + o - 1)
                    fn(tg[:, o % 2, :], take(base)[:, 0:NT], ACT.Tanh, scale=0.5).then_inc(act_freed, 1)
                squares(L, 1, dve_freed, lambda k: dve_jobs(L, "w_o", k + 1))

                fn(cvT.rearrange("p f r -> p (f r)"), take(base)[:, 0:20 * KF]).then_inc(act_freed, 1)
                std(L, 1)

                def gelu(f):
                    act_.wait_ge(conved, L * KF + f + 1)
                    if f >= 2:
                        act_.wait_ge(dve_freed, dve_jobs(L, "up", f - 1))
                    fn(tg[:, f % 2, :], cv[:, f % 2, :], ACT.Gelu_apprx_tanh).then_inc(ff_gelu, 1)

                for f in range(KF):
                    bank = take(base)
                    if f >= 2:
                        act_.wait_ge(conved, L * KF + f - 1)
                    fn(GX[:, f % 2, 2:2 + NT], bank[:, 0:NT]).then_inc(gate_copied, 1)
                    fn(gcol[:, f, :], bank[:, SEQ - 2:NT]).then_inc(act_freed, 1)
                    if f >= 1:
                        gelu(f - 1)
                gelu(KF - 1)
                for j in range(6):
                    w = P * min(4, KF - 4 * j)
                    fn(gp_rows[:, 4 * P * j:4 * P * j + w], take(base)[0:10, 0:w]).then_inc(act_freed, 1)
                squares(L, 2, dve_freed, lambda k: dve_jobs(L, "down", k + 1), range(KD - 1))
                for k in range(2):
                    fn(pT[:, k, :], take(base)[:, 0:NT]).then_inc(act_freed, 1)
                squares(L, 2, dve_freed, lambda k: dve_jobs(L, "down", k + 1), (KD - 1,))
                std(L, 2)
                for o in range(KD):
                    fn(plT[:, o, :], take(base)[:, 0:NT]).then_inc(act_freed, 1)
                for o in range(KD):
                    if o >= 2:
                        act_.wait_ge(h_done, L * KD + (KD + o - 1))
                    fn(tg[:, o % 2, :], take(base)[:, 0:NT], ACT.Tanh, scale=0.5).then_inc(act_freed, 1)
                assert n[0] == ACT_LAYER, n
            n[0] = 0
            for t in range(3):
                m = P if t < 2 else NB
                last = fn(xrows[0:m, t, 0:512], take(DEPTH * ACT_LAYER + ACT_PRO)[0:m, :]).then_inc(act_freed, 1)

        @block.vector
        def _(dve):
            n, step = [0], [0]

            def take(base):
                dve.wait_ge(dve_ready, base + (n[0] + 1))
                n[0] += 1
                return bankV[(n[0] - 1) % BANKS]

            def link(ins):
                step[0] += 1
                ins.then_inc(dve_step, 1)
                dve.wait_ge(dve_step, step[0])

            tt, ts, stt = dve.tensor_tensor, dve.tensor_scalar, dve.scalar_tensor_tensor
            MUL, ADD, SUB, MAX, MIN = ALU.mult, ALU.add, ALU.subtract, ALU.max, ALU.min

            dve.sem_inc(y_taken, 1)
            for k in range(1, KD, 2):
                ins = dve.tensor_copy(hT[:, k, :], take(0)[:, 0:NT])
                ins.then_inc(dve_freed, 1)
            dve.wait_ge(act_freed, ACT_PRO)
            dve.wait_ge(dve_freed, DVE_PRO)
            dve.sem_inc(h_done, KD)
            with dve.Fori(0, DEPTH) as L:
                n[0], step[0] = 0, 0
                dve.sem_clear(dve_step)
                base = L * DVE_LAYER + DVE_PRO

                def add_squares(i, k):
                    if k >= 1:
                        dve.wait_ge(squared, L * 3 * KD + (i * KD + k + 1))
                        ins = tt(xn[:, k, :], xn[:, k - 1, :], xn[:, k, :], ADD)
                        if k < KD - 1:
                            link(ins)
                        else:
                            ins.then_inc(added, 1)

                def norm(i):
                    take(base)
                    dve.wait_ge(std_ready, L * 3 + i + 1)
                    dve.reciprocal(rstd[:], rstd[:]).then_inc(dve_freed, 1)
                    dve.wait_ge(dve_freed, base + n[0])
                    for k in range(KD):
                        stt(xn[:, k, :], hT[:, k, :], prm[:, KD * i + k:KD * i + k + 1], rstd[:], MUL, MUL).then_inc(normed, 1)

                dve.wait_ge(params_in, L * 112 + 112)
                dve.tensor_copy(ssm_rows[:, 2, :].rearrange("p (g n) -> p g n", g=2),
                                dt_rows[:].unsqueeze(2).broadcast_to([ST, 2, NS_])).then_inc(dt_rows_ready, 1)
                dve.tensor_copy(prm[:], take(base)[:, 0:28 + 3 * ST]).then_inc(dve_freed, 1)
                dve.wait_ge(dve_freed, dve_jobs(L, "params", 1))
                ar, ai = prm[:, 28:28 + ST], prm[:, 28 + ST:28 + 2 * ST]
                dt, th, ma, mag, abr, abi, den, am1, zr, zi, t1, t2 = (sm[:, j, :] for j in range(12))
                dve.wait_ge(dt_ready, L + 1)
                tt(th, dt, ai, MUL)
                link(tt(ma, dt, ar, MUL))
                link(tt(ang[:, 0], th.unsqueeze(1).broadcast_to([P, 8, ST]), c_pow[:].unsqueeze(2).broadcast_to([P, 8, ST]), MUL))
                link(ts(ang[:, 1], ang[:, 0], INV2PI, ROUND, MUL, ADD))
                link(ts(ang[:, 1], ang[:, 1], -ROUND, None, ADD))
                for part in (PI2_A, PI2_B, PI2_C):
                    link(stt(ang[:, 0], ang[:, 1], -part, ang[:, 0], MUL, ADD))
                link(ts(ang[:, 0], ang[:, 0], 3.1415925, -3.1415925, MIN, MAX))
                stt(ang[:, 2], ang[:, 0], -1.0, ang[:, 0], MUL, MAX).then_inc(trig_arg, 1)

                norm(0)

                dve.wait_ge(trig_ready, L + 1)
                tt(abr, mag, cs[:, 0, 0, :], MUL)
                tt(abi, mag, cs[:, 1, 0, :], MUL)
                tt(den, ar, ar, MUL)
                link(tt(t1, ai, ai, MUL))
                tt(den, den, t1, ADD)
                link(ts(am1, abr, -1.0, None, ADD))
                dve.reciprocal(den, den)
                tt(zr, am1, ar, MUL)
                tt(zi, abi, ar, MUL)
                tt(t1, abi, ai, MUL)
                link(tt(t2, am1, ai, MUL))
                tt(zr, zr, t1, ADD)
                link(tt(zi, zi, t2, SUB))
                tt(zr, zr, den, MUL)
                link(tt(zi, zi, den, MUL))
                dve.wait_ge(smat_in, L * 64 + 64)
                for r in range(2):
                    last = tt(cpad[:, r], cst_c[:, r].unsqueeze(2).broadcast_to([P, 4, 2, NS_]),
                              c_rmask[:].unsqueeze(1).unsqueeze(3).broadcast_to([P, 4, 2, NS_]), MUL)
                last.then_inc(c_ready, 1)
                zrb, zib = (x.unsqueeze(2).broadcast_to([P, ST, GC]) for x in (zr, zi))
                tt(bw[:, 0], bst[:, 0], zrb, MUL)
                tt(bw[:, 1], bst[:, 1], zib, MUL)
                tt(bw[:, 2], bst[:, 1], zrb, MUL)
                link(tt(bw[:, 3], bst[:, 0], zib, MUL))
                tt(bw[:, 0], bw[:, 0], bw[:, 1], SUB)
                link(tt(bw[:, 2], bw[:, 2], bw[:, 3], ADD))
                for r in range(2):
                    last = tt(bpad[:, r], bw[:, 2 * r].unsqueeze(2).broadcast_to([P, ST, 2, GC]),
                              c_gmask[:].unsqueeze(1).unsqueeze(3).broadcast_to([P, ST, 2, GC]), MUL)
                last.then_inc(b_ready, 1)
                for r in range(2):
                    ts(CT[:, r].rearrange("p k c -> p (k c)"), take(base)[:], 1.0 - 2.0 * r, None, MUL).then_inc(dve_freed, 1)
                for r in range(2):
                    dve.tensor_copy(BT[:, r].rearrange("p k c -> p (k c)"), take(base)[:]).then_inc(dve_freed, 1)

                dve.wait_ge(act_freed, act_jobs(L, "u", 4))
                tt(upad[:], uT[:, :, SEQ:NT].unsqueeze(2).broadcast_to([P, 4, 4, NB]),
                   c_qmask[:].unsqueeze(1).unsqueeze(3).broadcast_to([P, 4, 4, NB]), MUL).then_inc(u_spread, 1)

                dve.tensor_copy(h0[:].rearrange("p r x -> p (r x)"), take(base)[:, 0:2 * P]).then_inc(dve_freed, 1)
                dve.wait_ge(dve_freed, dve_jobs(L, "h0", 1))
                bank = take(base)
                def over(x):
                    return x.unsqueeze(1).broadcast_to([P, NB, ST])
                def rows(x):
                    return x.rearrange("p (s i) -> p s i", s=NB)
                for r in range(2):
                    w = W1[:, r, 0:P], W2[:, r, 0:P]
                    tt(rows(w[0]), rows(h0[:, r]), over(abr), MUL)
                    link(tt(rows(w[1]), rows(h0[:, 1 - r]), over(abi), MUL))
                    link(tt(w[0], w[0], w[1], ADD if r else SUB))
                    last = tt(hs[:, r, :].rearrange("p (s i) -> p i s", s=NB), w[0].rearrange("p (s i) -> p i s", s=NB),
                              bank[:, P * r:P * r + P].rearrange("p (i s) -> p i s", s=NB), ADD)
                last.then_inc(dve_freed, 1)
                dve.wait_ge(dve_freed, base + n[0])

                for i in range(ST):
                    q = i // 2
                    bank = take(base)
                    if i % 2 == 0:
                        dve.wait_ge(rot_ready, L * (ST // 2) + q + 1)
                    bu = bank[:].rearrange("p (c t) -> p c t", c=2)
                    co, si = (rot[:, q % 2, j, i % 2, :].unsqueeze(1).broadcast_to([P, 2, SEQ]) for j in range(2))
                    tt(W1, bu, co, MUL)
                    tt(W2, bu, si, MUL).then_inc(dve_freed, 1)
                    dve.wait_ge(dve_freed, base + n[0])
                    tt(W1[:, 0], W1[:, 0], W2[:, 1], ADD)
                    link(tt(W1[:, 1], W1[:, 1], W2[:, 0], SUB))
                    for c in range(2):
                        last = dve.tensor_tensor_scan(G[:, c], mag[:, i:i + 1].broadcast_to([P, SEQ]), W1[:, c], 0.0, MUL, ADD)
                    link(last)
                    tt(W1, G, co, MUL)
                    last = tt(W2, G, si, MUL)
                    if i % 2:
                        last.then_inc(rot_used, 1)
                        dve.wait_ge(rot_used, L * (ST // 2) + q + 1)
                    else:
                        link(last)
                    if i >= 2:
                        dve.wait_ge(y_ready, L * ST + i - 1)
                    tt(HH[:, i % 2, 0], W1[:, 0], W2[:, 1], SUB)
                    link(tt(HH[:, i % 2, 1], W1[:, 1], W2[:, 0], ADD))
                    dve.tensor_copy(hfin[:, :, i:i + 1], HH[:, i % 2, :, SEQ - 1:SEQ]).then_inc(state_ready, 1)
                    if i % 4 == 3:
                        k = i // 4
                        dve.wait_ge(y_ready, L * ST + i + 1)
                        stt(uT[:, k, :], uT[:, k, :], prm[:, 24 + k:25 + k], bankY[:, 0:NT], MUL, ADD).then_inc(y_taken, 1)

                dve.wait_ge(more_in, L * 128 + 128)
                dve.wait_ge(act_freed, act_jobs(L, "pe", 1))

                def parts(t):
                    m = P if t < 2 else NB
                    return m, z[0:m, t, 0:QW].rearrange("p (h d) -> p h d", h=H), \
                        z[0:m, t, QW:1280].rearrange("p (j v g d) -> p j v g d", j=3, v=2, g=KV)[:, :, 0]

                for t in range(3):
                    m, zq, zk = parts(t)
                    w = PTf[0:m, 1024 * (t % 2):1024 * (t % 2) + 896]
                    tt(w[:, 0:QW].rearrange("p (h d) -> p h d", h=H), zq, zq, MUL)
                    link(tt(w[:, QW:896].rearrange("p (j g d) -> p j g d", j=3, g=KV), zk, zk, MUL))
                    link(dve.tensor_reduce(ss[0:m, t, :], w.rearrange("p (h d) -> p h d", d=HD), AX, ADD))
                ts(ss[:, 0:2, :], ss[:, 0:2, :], 1.0 / HD, EPS, MUL, ADD)
                ts(ss[0:NB, 2, :], ss[0:NB, 2, :], 1.0 / HD, EPS, MUL, ADD).then_inc(hvar_ready, 1)
                dve.wait_ge(gates_tanh, L + 1)
                ts(bg[:, 0:2, :], bg[:, 0:2, :], 0.5, 0.5, MUL, ADD)
                ts(bg[0:NB, 2, :], bg[0:NB, 2, :], 0.5, 0.5, MUL, ADD).then_inc(gates_ready, 1)
                dve.wait_ge(hstd_ready, L + 1)
                dve.reciprocal(ss[:, 0:2, :], ss[:, 0:2, :])
                link(dve.reciprocal(ss[0:NB, 2, :], ss[0:NB, 2, :]))
                for t in range(3):
                    m, zq, zk = parts(t)
                    tt(zq, zq, ss[0:m, t, 0:H].unsqueeze(2).broadcast_to([m, H, HD]), MUL)
                    link(tt(zk, zk, ss[0:m, t, H:14].rearrange("p (j g) -> p j g", j=3).unsqueeze(3).broadcast_to([m, 3, KV, HD]), MUL))
                    tt(zq, zq, gains[0:m, 0:1, :].broadcast_to([m, H, HD]), MUL)
                    link(tt(zk, zk, gains[0:m, 1:4, :].unsqueeze(2).broadcast_to([m, 3, KV, HD]), MUL))
                    qc, qs = (PTf[0:m, 512 * j:512 * j + 512].rearrange("p (h d) -> p h d", h=H) for j in range(2))
                    kc, ksn = (PTf[0:m, 1024 + 256 * j:1280 + 256 * j].rearrange("p (j g d) -> p j g d", j=2, g=KV) for j in range(2))
                    zk = zk[:, 1:3]
                    co, si = c_cos[0:m, t, :], c_sin[0:m, t, :]
                    hf = HD // 2
                    tt(qc, zq, co.unsqueeze(1).broadcast_to([m, H, HD]), MUL)
                    for a, b in ((0, hf), (hf, 0)):
                        tt(qs[:, :, a:a + hf], zq[:, :, b:b + hf], si[:, a:a + hf].unsqueeze(1).broadcast_to([m, H, hf]), MUL)
                    tt(kc, zk, co.unsqueeze(1).unsqueeze(1).broadcast_to([m, 2, KV, HD]), MUL)
                    for a, b in ((0, hf), (hf, 0)):
                        last = tt(ksn[:, :, :, a:a + hf], zk[:, :, :, b:b + hf],
                                  si[:, a:a + hf].unsqueeze(1).unsqueeze(1).broadcast_to([m, 2, KV, hf]), MUL)
                    link(last)
                    tt(zq, qc, qs, ADD)
                    tt(zk, kc, ksn, ADD).then_inc(roped, 1)

                bank = take(base)
                tt(g64[:], bank[0:64, 0:24].rearrange("p (h b) -> p h b", h=H), c_head[:].unsqueeze(2).broadcast_to([64, H, 3]), MUL).then_inc(dve_freed, 1)
                dve.wait_ge(dve_freed, base + n[0])
                link(dve.tensor_reduce(gg[:], g64[:].rearrange("p h b -> p b h"), AX, ADD))

                bank = take(base)
                for r, table in ((0, c_ccos), (1, c_csin)):
                    last = tt(kct[:, r].rearrange("p (s n) -> p s n", s=NSEQ), bank[:, 256 * r:256 * r + NSEQ * NCMP].rearrange("p (s n) -> p s n", s=NSEQ),
                              table[:].unsqueeze(1).broadcast_to([P, NSEQ, NCMP]), MUL)
                last.then_inc(dve_freed, 1)
                dve.wait_ge(dve_freed, base + n[0])
                kv_ = kct.rearrange("p r (s n) -> p r s n", s=NSEQ)
                tt(keys[:, :, CMP0:KEYS], kv_[:, 0, 0:NB], kv_[:, 1, 0:NB], ADD)
                tt(kcmp[:], kv_[:, 0, NB], kv_[:, 1, NB], ADD).then_inc(kcmp_ready, 1)

                ts(SS[:, 0:NEW0], take(base)[0:64, :], SCALE, None, MUL).then_inc(dve_freed, 1)
                ts(SS[:, NEW0:KEYS], take(base)[0:64, 0:KEYS - NEW0], SCALE, None, MUL).then_inc(dve_freed, 1)
                dve.wait_ge(dve_freed, base + n[0])
                dve.tensor_reduce(sq4[:, 0:2], SS[:, 0:NEW0].rearrange("p (b k) -> p b k", b=2), AX, MAX)
                link(dve.tensor_reduce(sq4[:, 2:3], SS[:, CMP0:KEYS], AX, MAX))
                link(tt(sq4[:, 0:2], sq4[:, 0:2], SS[:, NEW0:CMP0], MAX))
                ts(sq4[:, 4:7], sq4[:, 0:3], -1.0, None, MUL).then_inc(s_max, 1)
                sc = SP_.rearrange("p (t h) n -> p t h n", t=2)
                for g in range(KV):
                    bt = take(base)[:, 0:8 * NCMP].rearrange("p (t c n) -> p t c n", t=2, c=4)
                    for t in range(2):
                        last = stt(sc[:, t, 4 * g:4 * g + 4], bt[:, t], SCALE,
                                   c_cmask[:, 0, t, :].unsqueeze(1).broadcast_to([P, 4, NCMP]), MUL, ADD)
                    last.then_inc(dve_freed, 1)
                dve.wait_ge(dve_freed, base + n[0])
                link(dve.tensor_reduce(cmx[:], SP_, AX, MAX))
                tt(SP_, SP_, cmx[:].unsqueeze(2).broadcast_to([P, 16, NCMP]), SUB).then_inc(c_arg, 1)

                def scores(u):
                    t = u % 2
                    nk = P * (t + 1)
                    bank = take(base)
                    if u >= 4:
                        dve.wait_ge(act_ready, probs_turned(L, u - 4))
                    stt(S(u), bank[:, 0:2 * nk].rearrange("p (b k) -> p b k", b=2), SCALE,
                        c_mask[:, SEQ - nk:SEQ].unsqueeze(1).broadcast_to([P, 2, nk]), MUL, ADD).then_inc(dve_freed, 1)
                    dve.wait_ge(dve_freed, base + n[0])
                    dve.tensor_reduce(mx[:, u % 4, 0:2], S(u), AX, MAX, negate=True).then_inc(p_max, 1)

                def weigh(u):
                    idx, t = divmod(u, 2)
                    c, g = divmod(idx, 2)
                    h = 4 * g + c
                    nk = P * (t + 1)
                    dve.wait_ge(p_exp, L * 2 * H + u + 1)
                    f = sums[:, u % 4, 2:4]
                    link(dve.reciprocal(f, sums[:, u % 4, 0:2]))
                    link(tt(f, f, bg[:, t, 3 * h + 1:3 * h + 3], MUL))
                    tt(S(u), S(u), f.unsqueeze(2).broadcast_to([P, 2, nk]), MUL).then_inc(p_prob, 1)

                scores(0)
                dve.wait_ge(s_exp, L + 1)
                link(tt(sq4[:, 8:10], sq4[:, 8:10], SS[:, NEW0:CMP0], ADD))
                link(ts(sq4[:, 8:11], sq4[:, 8:11], 1e-30, None, MAX))
                link(dve.reciprocal(sq4[:, 12:15], sq4[:, 8:11]))
                tt(sq4[:, 12:14], sq4[:, 12:14], gg[:, 1:3], MUL)
                link(tt(sq4[:, 14:15], sq4[:, 14:15], gg[:, 0:1], MUL))
                link(tt(SS[:, NEW0:CMP0], SS[:, NEW0:CMP0], sq4[:, 12:14], MUL))
                sv = SS[:, 0:NEW0].rearrange("p (b k) -> p b k", b=2)
                tt(sv, sv, sq4[:, 12:14].unsqueeze(2).broadcast_to([64, 2, PAST]), MUL)
                ts(SS[:, CMP0:KEYS], SS[:, CMP0:KEYS], sq4[:, 14:15], None, MUL)
                for b in range(2):
                    last = ts(snew[:, b, :], c_diag[:], SS[:, NEW0 + b:NEW0 + b + 1], None, MUL)
                last.then_inc(s_prob, 1)
                scores(1)
                dve.wait_ge(c_exp, L + 1)
                for t in range(2):
                    last = tt(sc[:, t], sc[:, t], c_cmask[:, 1, t, :].unsqueeze(1).broadcast_to([P, H, NCMP]), MUL)
                link(last)
                link(dve.tensor_reduce(csum[:], SP_, AX, ADD))
                link(ts(csum[:], csum[:], 1e-30, None, MAX))
                link(dve.reciprocal(csum[:], csum[:]))
                link(tt(csum[:].rearrange("p (t h) -> p t h", t=2), csum[:].rearrange("p (t h) -> p t h", t=2),
                        bg[:, 0:2, 0:22:3], MUL))
                tt(SP_, SP_, csum[:].unsqueeze(2).broadcast_to([P, 16, NCMP]), MUL).then_inc(c_prob, 1)
                for u in range(2 * H):
                    if u + 2 < 2 * H:
                        scores(u + 2)
                    weigh(u)

                for o in range(KD):
                    stt(sg[:, 0, o, :], sg[:, 0, o, :], 1.0, take(base)[:, 0:NT], ADD, MUL).then_inc(dve_freed, 1)
                dve.wait_ge(dve_freed, base + n[0])
                for o in range(KD):
                    bank = take(base)
                    dve.wait_ge(act_freed, act_jobs(L, "glu", o + 1))
                    stt(cv[:, o % 2, :], tg[:, o % 2, :], 1.0, bank[:, 0:NT], ADD, MUL).then_inc(dve_freed, 1)
                    dve.wait_ge(dve_freed, base + n[0])
                    link(stt(cv[:, o % 2, :], sg[:, 1, o, :], 1.0, cv[:, o % 2, :], ADD, MUL))
                    stt(sg[:, 0, o, :], cv[:, o % 2, :], 0.5, sg[:, 0, o, :], MUL, ADD).then_inc(merged, 1)
                for o in range(KD):
                    stt(hT[:, o, :], take(base)[:, 0:NT], 0.5, hT[:, o, :], MUL, ADD).then_inc(dve_freed, 1)
                    add_squares(1, o - 1)
                add_squares(1, KD - 1)

                norm(1)
                dve.wait_ge(act_freed, act_jobs(L, "conv", 1))

                def conv(f):
                    dve.wait_ge(gate_copied, L * KF + f + 1)
                    if f >= 2:
                        dve.wait_ge(ff_gelu, L * KF + f - 1)
                    x, c = GX[:, f % 2, :], cv[:, f % 2, :]
                    tap = [cvT[:, f, 16 + j:17 + j] for j in range(4)]
                    old = cvT[:, f, 0:16].rearrange("p (s j) -> p s j", j=2)
                    link(ts(c, x[:, 2:2 + NT], tap[2], tap[3], MUL, ADD))
                    stt(c[:, 0:SEQ], x[:, 1:1 + SEQ], tap[1], c[:, 0:SEQ], MUL, ADD)
                    link(stt(c[:, SEQ:NT], old[:, :, 1], tap[1], c[:, SEQ:NT], MUL, ADD))
                    stt(c[:, 0:SEQ], x[:, 0:SEQ], tap[0], c[:, 0:SEQ], MUL, ADD)
                    stt(c[:, SEQ:NT], old[:, :, 0], tap[0], c[:, SEQ:NT], MUL, ADD).then_inc(conved, 1)

                def gated(f):
                    bank = take(base)
                    dve.wait_ge(ff_gelu, L * KF + f + 1)
                    tt(act[:, f, :], tg[:, f % 2, :], bank[:, 0:NT], MUL).then_inc(dve_freed, 1)

                for f in range(KF):
                    conv(f)
                    if f >= 1:
                        gated(f - 1)
                gated(KF - 1)
                for o in range(KD):
                    tt(hT[:, o, :], take(base)[:, 0:NT], hT[:, o, :], ADD).then_inc(dve_freed, 1)
                    add_squares(2, o - 1)
                add_squares(2, KD - 1)

                norm(2)
                for o in range(KD):
                    dve.wait_ge(act_freed, act_jobs(L, "ple_gate", o + 1))
                    link(stt(cv[:, o % 2, :], tg[:, o % 2, :], 1.0, plT[:, o, :], ADD, MUL))
                    stt(hT[:, o, :], cv[:, o % 2, :], 0.5, hT[:, o, :], MUL, ADD).then_inc(h_done, 1)
                assert n[0] == DVE_LAYER, n
            n[0] = 0
            for t in range(3):
                m = P if t < 2 else NB
                dve.tensor_copy(xrows[0:m, t, 512:D], take(DEPTH * DVE_LAYER + DVE_PRO)[0:m, :]).then_inc(dve_freed, 1)


def constants():
    import numpy as np
    f = np.float32
    half = HD // 2
    inv = (f(10000.0) ** (-np.arange(half, dtype=f) / f(half))).astype(f)

    def rot(pos):
        ang = pos.astype(f)[:, None] * inv[None, :]
        co, si = np.cos(ang).astype(f), np.sin(ang).astype(f)
        return np.concatenate([co, co], 1), np.concatenate([-si, si], 1)

    pos = np.arange(3 * P)
    pos[2 * P:] = PAST
    co, si = rot(pos)
    cend, send = rot(np.arange(NCMP) * CS + CB - 1)
    q, k = np.arange(P)[:, None], np.arange(P)[None, :]
    mask = np.concatenate([np.zeros((P, P), f), np.where(k <= q, 0, NEG).astype(f)], 1)
    seen = np.stack([(np.arange(NCMP) * CS + CB - 1)[None, :] <= q + P * t for t in range(2)], 1)
    row = np.arange(64)
    c = {
        "ident": np.eye(P), "mask": mask,
        "cos": co.reshape(3, P, HD).transpose(1, 0, 2), "sin": si.reshape(3, P, HD).transpose(1, 0, 2),
        "ccos": np.concatenate([cend.T, cend.T]), "csin": np.concatenate([send.T, send.T]),
        "cmask": np.stack([np.where(seen, 0, NEG), seen], 1),
        "ones": np.ones((P, P)),
        "gmask": np.stack([np.arange(P) < 64, np.arange(P) >= 64], 1),
        "rmask": np.stack([np.arange(P) // 16 % 2 == 0, np.arange(P) // 16 % 2 == 1], 1),
        "qmask": np.arange(P)[:, None] // 32 == np.arange(4)[None, :],
        "pow": np.tile(2.0 ** np.arange(8), (P, 1)),
        "sel": np.arange(NB)[:, None] == row[None, :] // 8,
        "diag": row[:, None] // 8 == np.arange(NB)[None, :],
        "head": row[:, None] % 8 == np.arange(8)[None, :],
        "bias": np.tile(np.array([EPS, np.pi / 2]), (P, 1)),
    }
    return {k: np.ascontiguousarray(v.astype(f)) for k, v in c.items()}


OUT_SHAPES = [(1, SEQ, D), (NB, 1, D)] + [(DEPTH, 1, SEQ, 2, KV, HD)] * 3 + [(DEPTH, 1, NG, NS_)] * 2 + \
    [(DEPTH, 1, 2, FF)] + [(DEPTH, NB, 1, 2, KV, HD)] * 2 + [(DEPTH, NB, PAST, 2, KV, HD)] + \
    [(DEPTH, NB, NG, NS_)] * 2 + [(DEPTH, NB, 2, FF)]


def kernel(**inputs):
    import numpy as np
    import concourse.bacc as bacc
    from concourse.bass_utils import run_bass_kernel_spmd as run

    nc = bacc.Bacc("TRN2", target_bir_lowering=False, num_devices=1)
    arrays, A, C, O = {}, {}, {}, []
    for name, value in inputs.items():
        a = np.ascontiguousarray(value)
        arrays[f"in_{name}_dram"] = a
        A[name] = nc.dram_tensor(f"in_{name}_dram", a.shape, mybir.dt.from_np(a.dtype), kind="ExternalInput").ap()
    for name, a in constants().items():
        arrays[f"c_{name}_dram"] = a
        C[name] = nc.dram_tensor(f"c_{name}_dram", a.shape, F32, kind="ExternalInput").ap()
    for i, shape in enumerate(OUT_SHAPES):
        O.append(nc.dram_tensor(f"out_{i}_dram", shape, F32, kind="ExternalOutput").ap())
    trunk(nc, A, C, O)
    r = run(nc, [arrays], core_ids=[0])
    return tuple(r.results[0][f"out_{i}_dram"] for i in range(len(OUT_SHAPES)))
```
